# Optimizing a Trainium2 kernel written in Bass

```python
import jax, jax.numpy as jnp
from jax import lax
import numpy as np

D_MODEL = 1024
BATCH = 1
SEQ = 256
DEPTH = 4
DEC_BATCH = 8
DEC_SEQ = 16
PAST_LEN = 256

CHUNK = 64
N_MIXERS = 3
N_FOX = (DEPTH + 2) // 3
N_HGRN = (DEPTH + 1) // 3
N_POOL = DEPTH // 3
FOX_HEADS = 16
FOX_HEAD_DIM = D_MODEL // FOX_HEADS
Q_BLOCK = 128
HGRN_HEADS = 8
HGRN_DK = D_MODEL // HGRN_HEADS
HGRN_DV = D_MODEL // HGRN_HEADS
POOL_WINDOWS = (2, 4, 8, 16)
POOL_GROUP = D_MODEL // len(POOL_WINDOWS)
POOL_HIST = max(POOL_WINDOWS) - 1
FFN_HIDDEN = ((8 * D_MODEL + 3 * 256 - 1) // (3 * 256)) * 256
ALPHA = (2 * DEPTH) ** 0.25
BETA = (8 * DEPTH) ** -0.25
LN_EPS = 1e-5
RMS_EPS = 1e-6

kernel_name = 'hybrid_fox_hgrn2_pool_streaming_step'

def layer_norm(x, g, b):
    xf = x.astype(jnp.float32)
    mu = jnp.mean(xf, axis=-1, keepdims=True)
    var = jnp.mean(jnp.square(xf - mu), axis=-1, keepdims=True)
    return ((xf - mu) * lax.rsqrt(var + LN_EPS) * g + b).astype(x.dtype)

def swiglu_ffn(x, w_in, w_out):
    a, u = jnp.split(x @ w_in, 2, axis=-1)
    return (jax.nn.silu(a) * u) @ w_out

def fox_project(x, w_in, b_f):
    B, T, _ = x.shape
    proj = x @ w_in
    hs = (B, T, FOX_HEADS, FOX_HEAD_DIM)
    q = proj[..., :D_MODEL].reshape(hs)
    k = proj[..., D_MODEL:2 * D_MODEL].reshape(hs)
    v = proj[..., 2 * D_MODEL:3 * D_MODEL].reshape(hs)
    lf = jax.nn.log_sigmoid((proj[..., 3 * D_MODEL:] + b_f).astype(jnp.float32))
    return q, k, v, lf

def fox_attend(q, k, v, cq, ck, qpos, kpos):
    s = jnp.einsum('bqhd,bkhd->bhqk', q, k).astype(jnp.float32) * (FOX_HEAD_DIM ** -0.5)
    s = s + jnp.swapaxes(cq, 1, 2)[:, :, :, None] - jnp.swapaxes(ck, 1, 2)[:, :, None, :]
    s = jnp.where(kpos[None, :] <= qpos[:, None], s, -jnp.inf)
    p = jax.nn.softmax(s, axis=-1).astype(v.dtype)
    return jnp.einsum('bhqk,bkhd->bqhd', p, v)

def fox_prompt(x, w_in, b_f, w_out):
    B, T, _ = x.shape
    q, k, v, lf = fox_project(x, w_in, b_f)
    c = jnp.cumsum(lf, axis=1)
    pos = jnp.arange(T)
    blocks = []
    for lo in range(0, T, Q_BLOCK):
        hi = min(lo + Q_BLOCK, T)
        blocks.append(fox_attend(q[:, lo:hi], k[:, :hi], v[:, :hi], c[:, lo:hi], c[:, :hi], pos[lo:hi], pos[:hi]))
    o = jnp.concatenate(blocks, axis=1).reshape(B, T, D_MODEL)
    return o @ w_out, k, v, lf

def fox_sample(x, cache_k, cache_v, cache_lf, w_in, b_f, w_out):
    B, T, _ = x.shape
    P = cache_k.shape[1]
    q, k, v, lf = fox_project(x, w_in, b_f)
    k_all = jnp.concatenate([cache_k.astype(k.dtype), k], axis=1)
    v_all = jnp.concatenate([cache_v.astype(v.dtype), v], axis=1)
    c = jnp.cumsum(jnp.concatenate([cache_lf.astype(jnp.float32), lf], axis=1), axis=1)
    kpos = jnp.arange(P + T)
    o = fox_attend(q, k_all, v_all, c[:, P:], c, kpos[P:], kpos)
    return o.reshape(B, T, D_MODEL) @ w_out, k, v, lf

def hgrn_chunk_step(S, inp):
    q, k, v, g = inp
    L = q.shape[1]
    b = jnp.cumsum(g, axis=1)
    causal = jnp.arange(L)[:, None] >= jnp.arange(L)[None, :]
    diff = b[:, :, None] - b[:, None, :]
    decay = jnp.exp(jnp.where(causal[None, :, :, None, None], diff, -jnp.inf))
    scores = jnp.einsum('bthc,bshc,btshc->bhts', q, k, decay)
    o = jnp.einsum('bhts,bshv->bthv', scores, v) + jnp.einsum('bthc,bhcv->bthv', q * jnp.exp(b), S)
    b_last = b[:, -1]
    S_new = jnp.exp(b_last)[..., None] * S + jnp.einsum('bshc,bshv->bhcv', k * jnp.exp(b_last[:, None] - b), v)
    return S_new, o

def hgrn_mix(x, S0, w_in, lb, norm_g, w_out):
    B, T, _ = x.shape
    q, fx, iv, gate = jnp.split(x @ w_in, 4, axis=-1)
    ks = (B, T, HGRN_HEADS, HGRN_DK)
    q = jax.nn.silu(q.astype(jnp.float32)).reshape(ks)
    fx = fx.astype(jnp.float32).reshape(ks)
    lb = lb.reshape(HGRN_HEADS, HGRN_DK)
    log_f = jnp.log(lb + (1.0 - lb) * jax.nn.sigmoid(fx))
    k = (1.0 - lb) * jax.nn.sigmoid(-fx)
    v = iv.astype(jnp.float32).reshape(B, T, HGRN_HEADS, HGRN_DV)
    L = CHUNK if T % CHUNK == 0 else T
    n = T // L
    to_chunks = lambda a: jnp.moveaxis(a.reshape((B, n, L) + a.shape[2:]), 1, 0)
    S_final, o = lax.scan(hgrn_chunk_step, S0.astype(jnp.float32),
                          (to_chunks(q), to_chunks(k), to_chunks(v), to_chunks(log_f)))
    o = jnp.moveaxis(o, 0, 1).reshape(B, T, HGRN_HEADS, HGRN_DV)
    o = o * lax.rsqrt(jnp.mean(jnp.square(o), axis=-1, keepdims=True) + RMS_EPS) * norm_g
    o = o.reshape(B, T, D_MODEL) * jax.nn.silu(gate.astype(jnp.float32))
    return o.astype(x.dtype) @ w_out, S_final

def pool_mix(x, hist, pos, w_pool, scale):
    B, T, _ = x.shape
    ext = jnp.concatenate([hist.astype(x.dtype), x], axis=1)
    xf = ext.astype(jnp.float32)
    csum = jnp.concatenate([jnp.zeros((B, 1, D_MODEL), jnp.float32), jnp.cumsum(xf, axis=1)], axis=1)
    end = POOL_HIST + 1
    groups = []
    for gi, w in enumerate(POOL_WINDOWS):
        sl = slice(gi * POOL_GROUP, (gi + 1) * POOL_GROUP)
        cs = csum[:, :, sl]
        window_sum = cs[:, end:end + T] - cs[:, end - w:end - w + T]
        count = jnp.minimum(pos + 1, w).astype(jnp.float32)[None, :, None]
        groups.append(window_sum / count - xf[:, POOL_HIST:, sl])
    z = jnp.stack(groups, axis=2)
    y = jnp.einsum('btgc,gcd->btgd', z, w_pool.astype(jnp.float32)).reshape(B, T, D_MODEL) * scale
    return y.astype(x.dtype), ext[:, -POOL_HIST:]

def setup_inputs(seed: int = 0) -> dict:
    key = jax.random.key(seed)
    ks = jax.random.split(key, 20)
    nrm = lambda k, shape, s: s * jax.random.normal(k, shape, jnp.float32)
    return {
        'x_prompt': nrm(ks[0], (BATCH, SEQ, D_MODEL), 1.0),
        'x_sample': nrm(ks[1], (DEC_BATCH, DEC_SEQ, D_MODEL), 1.0),
        'cache_fox_k': nrm(ks[2], (N_FOX, DEC_BATCH, PAST_LEN, FOX_HEADS, FOX_HEAD_DIM), 1.0),
        'cache_fox_v': nrm(ks[3], (N_FOX, DEC_BATCH, PAST_LEN, FOX_HEADS, FOX_HEAD_DIM), 1.0),
        'cache_fox_lf': jax.nn.log_sigmoid(3.0 + jax.random.normal(ks[4], (N_FOX, DEC_BATCH, PAST_LEN, FOX_HEADS), jnp.float32)),
        'state_hgrn': nrm(ks[5], (N_HGRN, DEC_BATCH, HGRN_HEADS, HGRN_DK, HGRN_DV), 0.3),
        'cache_pool': nrm(ks[6], (N_POOL, DEC_BATCH, POOL_HIST, D_MODEL), 1.0),
        'w_fox_in': nrm(ks[7], (N_FOX, D_MODEL, 3 * D_MODEL + FOX_HEADS), D_MODEL ** -0.5),
        'b_fox_f': 1.0 + 5.0 * jax.random.uniform(ks[8], (N_FOX, FOX_HEADS), jnp.float32),
        'w_fox_out': nrm(ks[9], (N_FOX, D_MODEL, D_MODEL), BETA * D_MODEL ** -0.5),
        'w_hgrn_in': nrm(ks[10], (N_HGRN, D_MODEL, 4 * D_MODEL), D_MODEL ** -0.5),
        'hgrn_lb': nrm(ks[11], (DEPTH, HGRN_HEADS * HGRN_DK), 1.0),
        'hgrn_norm_g': 1.0 + nrm(ks[12], (N_HGRN, HGRN_DV), 0.1),
        'w_hgrn_out': nrm(ks[13], (N_HGRN, D_MODEL, D_MODEL), BETA * D_MODEL ** -0.5),
        'w_pool': nrm(ks[14], (N_POOL, len(POOL_WINDOWS), POOL_GROUP, POOL_GROUP), BETA * POOL_GROUP ** -0.5),
        'pool_scale': 1.0 + nrm(ks[15], (N_POOL, D_MODEL), 0.1),
        'w_ffn_in': nrm(ks[16], (DEPTH, D_MODEL, 2 * FFN_HIDDEN), D_MODEL ** -0.5),
        'w_ffn_out': nrm(ks[17], (DEPTH, FFN_HIDDEN, D_MODEL), BETA * FFN_HIDDEN ** -0.5),
        'ln_g': 1.0 + nrm(ks[18], (DEPTH, 2, D_MODEL), 0.1),
        'ln_b': nrm(ks[19], (DEPTH, 2, D_MODEL), 0.05),
    }

def reference(x_prompt, x_sample, cache_fox_k, cache_fox_v, cache_fox_lf, state_hgrn, cache_pool,
              w_fox_in, b_fox_f, w_fox_out, w_hgrn_in, hgrn_lb, hgrn_norm_g, w_hgrn_out,
              w_pool, pool_scale, w_ffn_in, w_ffn_out, ln_g, ln_b):
    lb_sched = jnp.cumsum(jax.nn.softmax(hgrn_lb.astype(jnp.float32), axis=0), axis=0)
    lb_sched = lb_sched - lb_sched[0]
    xp, xs = x_prompt, x_sample
    Bp, Tp, _ = xp.shape
    Bs, Ts, _ = xs.shape
    pos_p = jnp.arange(Tp)
    pos_s = PAST_LEN + jnp.arange(Ts)
    fk_p, fv_p, flf_p, hs_p, pl_p = [], [], [], [], []
    fk_s, fv_s, flf_s, hs_s, pl_s = [], [], [], [], []
    for i in range(DEPTH):
        j = i // N_MIXERS
        kind = i % N_MIXERS
        if kind == 0:
            mp, kp, vp, lfp = fox_prompt(xp, w_fox_in[j], b_fox_f[j], w_fox_out[j])
            ms, ks_, vs, lfs = fox_sample(xs, cache_fox_k[j], cache_fox_v[j], cache_fox_lf[j],
                                          w_fox_in[j], b_fox_f[j], w_fox_out[j])
            fk_p.append(kp); fv_p.append(vp); flf_p.append(lfp)
            fk_s.append(ks_); fv_s.append(vs); flf_s.append(lfs)
        elif kind == 1:
            S0 = jnp.zeros((Bp, HGRN_HEADS, HGRN_DK, HGRN_DV), jnp.float32)
            mp, sp = hgrn_mix(xp, S0, w_hgrn_in[j], lb_sched[i], hgrn_norm_g[j], w_hgrn_out[j])
            ms, ss = hgrn_mix(xs, state_hgrn[j], w_hgrn_in[j], lb_sched[i], hgrn_norm_g[j], w_hgrn_out[j])
            hs_p.append(sp); hs_s.append(ss)
        else:
            hist0 = jnp.zeros((Bp, POOL_HIST, D_MODEL), xp.dtype)
            mp, pp = pool_mix(xp, hist0, pos_p, w_pool[j], pool_scale[j])
            ms, ps = pool_mix(xs, cache_pool[j], pos_s, w_pool[j], pool_scale[j])
            pl_p.append(pp); pl_s.append(ps)
        xp = layer_norm(ALPHA * xp + mp, ln_g[i, 0], ln_b[i, 0])
        xs = layer_norm(ALPHA * xs + ms, ln_g[i, 0], ln_b[i, 0])
        xp = layer_norm(ALPHA * xp + swiglu_ffn(xp, w_ffn_in[i], w_ffn_out[i]), ln_g[i, 1], ln_b[i, 1])
        xs = layer_norm(ALPHA * xs + swiglu_ffn(xs, w_ffn_in[i], w_ffn_out[i]), ln_g[i, 1], ln_b[i, 1])
    return (xp, xs,
            jnp.stack(fk_p), jnp.stack(fv_p), jnp.stack(flf_p), jnp.stack(hs_p), jnp.stack(pl_p),
            jnp.stack(fk_s), jnp.stack(fv_s), jnp.stack(flf_s), jnp.stack(hs_s), jnp.stack(pl_s))


_drawn_inputs = setup_inputs


def setup_inputs(seed=0):
    import zlib

    import numpy as np

    out = dict(_drawn_inputs(seed))
    spreads = {}
    factors = {'cache_fox_lf': 4.432, 'state_hgrn': 4.258, 'hgrn_norm_g': 3.907}
    for name, (base, spread) in spreads.items():
        noise = np.random.default_rng([zlib.crc32(name.encode()), seed]).standard_normal(out[name].shape)
        drawn = base * np.exp(spread * noise) if base else spread * noise
        out[name] = __import__('jax').numpy.asarray(drawn.astype(out[name].dtype))
    for name, factor in factors.items():
        out[name] = (out[name] * factor).astype(out[name].dtype)
    return out
```

```python
from contextlib import ExitStack

import concourse.bass as bass
from concourse import mybir

F32 = mybir.dt.float32
F32R = mybir.dt.float32r
I32 = mybir.dt.int32
ALU = mybir.AluOpType
ACT = mybir.ActivationFunctionType
AX_X = mybir.AxisListType.X

D = 1024
P = 128
KD = D // P
SEQ, DB, DT, PAST = 256, 8, 16, 256
NTOK = 3
T = NTOK * P
DEPTH = 4
KINDS = ("fox", "hgrn", "pool")
HEADS, HD = 16, 64
HG = 8
HIST = 15
FF = ((8 * D + 3 * 256 - 1) // (3 * 256)) * 256
KF = FF // P
ALPHA = (2 * DEPTH) ** 0.25
SCALE = HD ** -0.5
LN_EPS, RMS_EPS = 1e-5, 1e-6
MASKED = -1e30
NEWTON = 3
RSQRT = 3 + 3 * NEWTON

RING = 4
WCOLS = 512
CU = D // (2 * P)
CF = KF // 2

LEVELS = (1, 2, 4, 8, 16, 32, 64)
LCOLS = [T if 2 * m <= DT else SEQ for m in LEVELS]
LOFF = [sum(LCOLS[:n]) for n in range(len(LEVELS))]
LALL = sum(LCOLS)
TILE_LEVELS = (7, 7, 4)


def phase_starts():
    starts, n = [], 0
    for i in range(DEPTH):
        kind = KINDS[i % 3]
        s = {"mix": n}
        n += {"fox": 6 * CU, "hgrn": 8 * CU, "pool": 0}[kind]
        s["out"] = n
        n += 2 if kind == "pool" else 2 * CU
        s["up"] = n
        n += CF * CU
        s["down"] = n
        n += 2 * CF
        starts.append(s)
    return starts, n


def trunk_program(nc, x_prompt, x_sample, cache_fox_k, cache_fox_v, cache_fox_lf, state_hgrn, cache_pool,
                  w_fox_in, b_fox_f, w_fox_out, w_hgrn_in, hgrn_lb, hgrn_norm_g, w_hgrn_out,
                  w_pool, pool_scale, w_ffn_in, w_ffn_out, ln_g, ln_b,
                  y_prompt, y_sample, fox_k_prompt, fox_v_prompt, fox_lf_prompt, hgrn_state_prompt, pool_prompt,
                  fox_k_sample, fox_v_sample, fox_lf_sample, hgrn_state_sample, pool_sample):
    ds = bass.ds
    START, UNITS = phase_starts()
    LN_LAST = 2 * DEPTH - 1

    with ExitStack() as ctx:
        place = {}

        def sb(name, shape, offset, dt=F32):
            size = 4
            for s in shape[1:]:
                size *= s
            size = -(-size // 32) * 32
            place[name] = offset + size
            return nc.alloc_sbuf_tensor_at(name, shape, dt, offset=offset)

        def after(name):
            return place[name]

        def sem(name):
            return ctx.enter_context(nc.semaphore(name))

        base = -(-nc.sbuf_base // 64) * 64
        w_raw = sb("w_raw", [P, RING, 2 * WCOLS], base)
        w_hi = sb("w_hi", [P, RING, 2 * WCOLS], after("w_raw"), F32R)
        w_lo = sb("w_lo", [P, RING, 2 * WCOLS], after("w_hi"), F32R)
        x_tok = sb("x_tok", [P, NTOK, D], after("w_lo"))
        gb = sb("gb", [P, 2, D], after("x_tok"))
        ident = sb("ident", [P, P], after("gb"))
        causal = sb("causal", [P, P], after("ident"))
        new_mask = sb("new_mask", [P, DT], after("causal"))
        half = sb("half", [P, 2], after("new_mask"))
        gbT = sb("gbT", [P, KD, 4 * DEPTH], after("half"))
        lbT = sb("lbT", [P, KD, DEPTH], after("gbT"))
        lb_col = sb("lb_col", [P, KD], after("lbT"))
        oml_col = sb("oml_col", [P, KD], after("lb_col"))
        lb_max = sb("lb_max", [P, KD], after("oml_col"))
        lb_sum = sb("lb_sum", [P, KD], after("lb_max"))
        stats = sb("stats", [P, NTOK, 2, 6], after("lb_sum"))
        mv = sb("mv", [P, NTOK, 2], after("stats"))
        rstd = sb("rstd", [P, NTOK], after("mv"))
        var = sb("var", [P, NTOK], after("rstd"))
        nt = sb("nt", [P, NTOK], after("var"))
        t32 = sb("t32", [P, 2, T], after("nt"))
        xT_hi = sb("xT_hi", [P, KD, T], after("t32"), F32R)
        xT_lo = sb("xT_lo", [P, KD, T], after("xT_hi"), F32R)
        xn = sb("xn", [P, NTOK, D], after("xT_lo"))
        qT = sb("qT", [P, KD, T], after("xT_lo"))
        u0 = after("xn")
        hT_hi = sb("hT_hi", [P, KF, T], u0, F32R)
        hT_lo = sb("hT_lo", [P, KF, T], after("hT_hi"), F32R)
        sg = sb("sg", [P, 2, 2, T], after("hT_lo"))
        h32 = sb("h32", [P, 2, 2, T], after("sg"))
        kT = sb("kT", [P, KD, T], u0)
        kv_tok = sb("kv_tok", [P, 2, NTOK, D], after("kT"))
        o_tok = kv_tok[:, 0, 0:2, :]
        craw = sb("craw", [HEADS, DB, PAST + DT], after("kv_tok"))
        cp = sb("cp", [HEADS, SEQ], after("craw"))
        wf = sb("wf", [P, KD, HEADS], after("cp"))
        wf_hi = sb("wf_hi", [P, KD, HEADS], after("wf"), F32R)
        wf_lo = sb("wf_lo", [P, KD, HEADS], after("wf_hi"), F32R)
        heads8 = sb("heads8", [HEADS, 2, P], after("wf"))
        bf = sb("bf", [P, HEADS], after("wf_lo"))
        z = sb("z", [P, NTOK, HEADS], after("bf"))
        za = sb("za", [P, NTOK, HEADS], after("z"))
        zm = sb("zm", [P, NTOK, HEADS], after("za"))
        lf_tok = sb("lf_tok", [P, NTOK, HEADS], after("zm"))
        lfc = sb("lfc", [P, DB * 2, HEADS], after("lf_tok"))
        qbd = sb("qbd", [P, 2, KD, 2, DT], after("lfc"))
        k_new = sb("k_new", [P, 2, KD, DT], after("qbd"))
        p_s = sb("p_s", [P, 2, T], after("k_new"))
        pT_s = sb("pT_s", [P, 2, T], after("p_s"))
        mx = sb("mx", [P, 4, 2], after("pT_s"))
        nmx = sb("nmx", [P, 4, 2], after("mx"))
        rs = sb("rs", [P, 4, 2], after("nmx"))
        rt = sb("rt", [P, 4], after("rs"))
        rcp = sb("rcp", [P, 4, 2], after("rt"))
        k_c0 = sb("k_c0", [P, 2, D], after("rcp"))
        v_c0 = sb("v_c0", [P, 2, D], after("k_c0"))
        k_c1 = sb("k_c1", [P, 2, D], after("v_c0"))
        v_c1 = sb("v_c1", [P, 2, D], after("k_c1"))
        ktc = sb("ktc", [P, KD, PAST], after("v_c1"))
        ones = sb("ones", [HEADS, PAST + DT], after("v_c1"))
        k_c, v_c = (k_c0, k_c1), (v_c0, v_c1)
        q_s = sb("q_s", [P, 4, SEQ], after("v_c0"))
        sel = sb("sel", [HEADS, 4, P], after("q_s"))
        p_p = sb("p_p", [P, 4, T], after("sel"))
        pT_p = sb("pT_p", [P, 2, T], after("p_p"))
        sp = sb("sp", [P, HG, T], u0)
        sn = sb("sn", [P, HG, T], after("sp"))
        vg = sb("vg", [P, 2, NTOK, D], after("sn"))
        S_b = sb("S_b", [P, 2, DB, P], after("vg"))
        b_h = sb("b_h", [P, T], after("S_b"))
        k_h = sb("k_h", [P, T], after("b_h"))
        e_b = sb("e_b", [P, T], after("k_h"))
        e_l = sb("e_l", [P, T], after("e_b"))
        q_e = sb("q_e", [P, T], after("e_l"))
        k2 = sb("k2", [P, T], after("q_e"))
        k2T = sb("k2T", [P, T], after("k2"))
        q_blk = sb("q_blk", [P, DB, P], after("k2T"))
        v_m = sb("v_m", [P, DB, P], after("q_blk"))
        s1 = sb("s1", [P, P], after("v_m"))
        s_fin = sb("s_fin", [P, 2, P], after("s1"))
        ng = sb("ng", [P, P], after("s_fin"))
        row_m = sb("row_m", [P, DB], after("ng"))
        cut = sb("cut", [P, T], after("row_m"))
        lmask = sb("lmask", [P, 8, P], after("cut"))
        ss = sb("ss", [P, NTOK], after("lmask"))
        rr = sb("rr", [P, NTOK], after("ss"))
        sq = sb("sq", [P, P], after("rr"))
        lev = sb("lev", [P, LALL], after("t32"))
        sc = sb("sc", [P, 2, 8, P], after("lev"))
        assert after("sc") <= after("xT_lo")
        ext_p = sb("ext_p", [P, KD, HIST + SEQ], u0)
        ext_s = sb("ext_s", [P, KD, DB, HIST + DT], after("ext_p"))
        wp = [sb(f"wp{n}", [P, 2, HIST + SEQ], after("ext_s") if n == 0 else after(f"wp{n-1}")) for n in range(2)]
        ws = [sb(f"ws{n}", [P, 2, DB, HIST + DT], after("wp1") if n == 0 else after(f"ws{n-1}")) for n in range(2)]
        zp = sb("zp", [P, KD, T], after("ws1"))
        cnt = sb("cnt", [P, DT], after("zp"))
        scale_bc = sb("scale_bc", [P, D], after("cnt"))
        hist = sb("hist", [DB * HIST, D], after("scale_bc"))
        zq = sb("zq", [P, 2, DT], after("hist"))
        ysc = sb("ysc", [P, 2, WCOLS], after("zq"))
        for name, end in place.items():
            assert end <= nc.sbuf_usable_end, (name, end, nc.sbuf_usable_end)
        gb_rows = sb("gb_rows", [4 * DEPTH, D], u0)
        lb_rows = sb("lb_rows", [DEPTH, D], after("gb_rows"))

        ps = ctx.enter_context(nc.psum_tensor("ps", [P, 8, 512], F32))

        raw_loaded = [sem(f"raw_loaded{n}") for n in range(RING)]
        hi_ready = sem("hi_ready")
        lo_ready = sem("lo_ready")
        unit_used = sem("unit_used")
        x_loaded = sem("x_loaded")
        rows_loaded = sem("rows_loaded")
        const_set = sem("const_set")
        mask_loaded = sem("mask_loaded")
        ident_ready = sem("ident_ready")
        rowsT_done = sem("rowsT_done")
        gbT_ready = sem("gbT_ready")
        lb_steps = sem("lb_steps")
        gb_loaded = sem("gb_loaded")
        def marks(prefix, turns, counts, skipped=()):
            sems = {k: sem(f"{prefix}_{k}") for k in counts}
            return [{k: (sems[k], sum(c for m in range(n) if (k, m) not in skipped)) for k, c in counts.items()}
                    for n in range(turns)]

        def at(mark, value):
            return mark[0], value + mark[1]

        LN = marks("ln", 2 * DEPTH, {"resid": 2 * NTOK, "stat": NTOK, "aggr": NTOK, "rstd": RSQRT, "xn": NTOK,
                                     "gx": NTOK, "x": NTOK})
        pooled = [2 * i for i in range(DEPTH) if KINDS[i % 3] == "pool"]
        TR = marks("tr", 2 * DEPTH, {"done": KD, "t32": KD, "hi": KD, "lo": KD},
                   [(k, n) for k in ("t32", "hi", "lo") for n in pooled])
        FFN = marks("ffn", DEPTH, {k: CF for k in ("silu", "h32", "hi", "lo")})
        fox_layers = [i for i in range(DEPTH) if KINDS[i % 3] == "fox"]
        FOX = dict(zip(fox_layers, marks("fox", len(fox_layers), {
            "wf_in": 16, "bf_in": 16, "lfc_in": 16, "wf_hi": 1, "wf_lo": 1, "ev_act": 3, "ev_dve": 3, "fproj": 1, "z": 1,
            "zma": 2, "ze": 1, "zl": 1, "lf": 1, "kT_done": KD, "kT_a": KD // 2, "kT_d": KD // 2, "lfT_done": 1,
            "ones": 1, "heads8": 1, "c_raw": 3, "c": 1 + DB, 
            **{k: HEADS for k in ("staged", "scores", "max", "nmax", "exp", "rcp", "pT", "pT_ev", "o", "o_ev")},
            "oT": KD, "oT_32": KD, "oT_hi": KD, "oT_lo": KD, "kv0": 32 * (DB // 2), "kv1": 32 * (DB // 2), "qst": DB,
            **{k: 2 * DB for k in ("ktr", "kt_a", "kt_d", "s_scores", "s_max", "s_nmax", "s_exp", "s_sum", "s_rcp",
                                   "s_p", "s_pT", "s_pT_ev", "s_o", "s_o_hi", "s_o_lo")},
            "stored": 16 * 6})))
        HGR = {i: {k: (sem(f"hgrn_{k}"), 0) for k in (
            "consts", "pconst", "masks", "ng_in", "ev", "gate", "g", "k", "b", "sub", "abs", "expl", "expb", "lq", "qe",
            "k2", "k2T", "k2T_ev", "qb", "vm", "sc", "scm", "s1", "s1_ev", "sfin", "sfin_ev", "o", "ss", "rr", "out",
            "st0_in", "st1_in", "upd", "snew", "stored0", "stored1", "pstored0", "pstored1", "oT", "oT_32", "oT_hi", "oT_lo")}
            for i in range(DEPTH) if KINDS[i % 3] == "hgrn"}
        POOL = {i: {k: (sem(f"pool_{k}"), 0) for k in (
            "in", "consts", "hist_T", "hist_ev", "ext", "w", "z", "hi", "lo", "ysc", "stored")}
            for i in range(DEPTH) if KINDS[i % 3] == "pool"}
        y_stored = sem("y_stored")

        block = ctx.enter_context(nc.Block())

        def iv(x):
            return isinstance(x, int)

        @block.sync
        def _(sync):
            def load(m, c, parts):
                if not iv(c) or m + CU * c >= RING:
                    sync.wait_ge(lo_ready, CU * c + (m - RING + 1))
                for kk in range(2):
                    dst, src = parts(kk)
                    sync.dma_start(dst, src).then_inc(raw_loaded[m % RING], 16)

            def square(w, m, c, u, cols):
                slot = m % RING
                rows = w.rearrange("(u kk p) n -> u kk p n", kk=2, p=P)
                load(m, c, lambda kk: (w_raw[:, slot, kk * WCOLS:(kk + 1) * WCOLS], rows[u, kk, :, ds(cols, WCOLS)]))

            def chunks(w, m0, n):
                first = 0
                if m0 == 0:
                    for u in range(CU):
                        square(w, u, 0, u, 0)
                    first = 1
                with sync.Fori(first, n) as c:
                    for u in range(CU):
                        square(w, m0 + u, c, u, c * WCOLS)

            for i in range(DEPTH):
                kind, j, s = KINDS[i % 3], i // 3, START[i]
                if kind == "fox":
                    chunks(w_fox_in[j], s["mix"], 6)
                    chunks(w_fox_out[j], s["out"], 2)
                elif kind == "hgrn":
                    chunks(w_hgrn_in[j], s["mix"], 8)
                    chunks(w_hgrn_out[j], s["out"], 2)
                else:
                    for u in range(2):
                        m = s["out"] + u
                        load(m, 0, lambda kk: (
                            w_raw[:, m % RING, kk * WCOLS:(kk + 1) * WCOLS].rearrange("p (g c) -> p g c", g=2),
                            w_pool[j, 2 * u:2 * u + 2, kk * P:(kk + 1) * P, :].rearrange("g p c -> p g c")))
                up = w_ffn_in[i].rearrange("(u kk p) (a n) -> u kk p a n", kk=2, p=P, a=2)
                with sync.Fori(0, CF) as c:
                    for u in range(CU):
                        slot = (s["up"] + u) % RING
                        load(s["up"] + u, c, lambda kk: (
                            w_raw[:, slot, kk * WCOLS:(kk + 1) * WCOLS].rearrange("p (a n) -> p a n", a=2),
                            up[u, kk, :, :, ds(c * 256, 256)]))
                for h in range(2):
                    for u in range(CF):
                        square(w_ffn_out[i], s["down"] + h * CF + u, 0, u, h * WCOLS)

        @block.scalar
        def _(act):
            def w_hi_of(m, c=0):
                if iv(c) and m + CU * c >= UNITS:
                    return
                slot = m % RING
                act.wait_ge(raw_loaded[slot], 32 * c + 32 * (m // RING + 1))
                if not iv(c) or m + CU * c >= RING:
                    act.wait_ge(unit_used, CU * c + (m - RING + 1))
                nc.scalar.activation(w_hi[:, slot, :], w_raw[:, slot, :], ACT.Copy).then_inc(hi_ready, 1)

            def ahead(m0, c=0):
                for u in range(CU):
                    w_hi_of(m0 + RING + u, c)

            def transposed(done, t32_at, lo, n=0, width=T, affine=False):
                for k in range(KD):
                    act.wait_ge(*at(done, k + 1))
                    if k >= 2:
                        act.wait_ge(*at(lo, k - 1))
                    nc.scalar.activation(t32[:, k % 2, 0:width], ps[:, k, 0:width], ACT.Identity,
                                         bias=gbT[:, k, n + 2 * DEPTH - 1:n + 2 * DEPTH] if affine else 0.0,
                                         scale=gbT[:, k, n - 1:n] if affine else 1.0).then_inc(t32_at[0], 1)

            def ffn(i):
                f, m0 = FFN[i], START[i]["up"]

                def chunk(c, k):
                    ahead(m0, c)
                    act.wait_ge(unit_used, CU * c + (m0 + CU))
                    if not (iv(c) and c < 2):
                        act.wait_ge(*at(f["h32"], c - 1))
                    nc.scalar.activation(sg[:, k], ps[:, 4 * k:4 * k + 2, 0:T], ACT.Silu).then_inc(f["silu"][0], 1)
                    act.wait_ge(*at(f["h32"], c + 1))
                    nc.scalar.activation(hT_hi[:, ds(2 * c, 2), :], h32[:, k], ACT.Copy).then_inc(f["hi"][0], 1)

                chunk(0, 0)
                chunk(1, 1)
                with act.Fori(2, CF - 1, 2) as c:
                    chunk(c, 0)
                    chunk(c + 1, 1)
                chunk(CF - 1, 0)
                for u in range(2 * CF):
                    w_hi_of(START[i]["down"] + u + RING)

            def fox(i, j):
                f, m0 = FOX[i], START[i]["mix"]
                ahead(m0)
                act.wait_ge(unit_used, m0 + CU)
                if i:
                    act.wait_ge(*at(LN[2 * i - 1]["x"], NTOK))
                nc.scalar.activation(qT[:, 0:4, :], ps[:, 0:4, 0:T], ACT.Copy).then_inc(f["ev_act"][0], 1)
                act.wait_ge(*at(f["wf_in"], 16))
                nc.scalar.activation(wf_hi[:, :, :], wf[:, :, :], ACT.Copy).then_inc(f["wf_hi"][0], 1)
                ahead(m0 + CU)
                with act.Fori(0, 2) as w:
                    for h in range(2):
                        for u in range(CU):
                            w_hi_of(m0 + (2 + h) * CU + RING + u, 2 * w)
                        if h == 0:
                            act.wait_ge(unit_used, 2 * CU * w + (m0 + 3 * CU))
                            nc.scalar.activation(kv_tok[:, ds(w, 1), :, 0:WCOLS],
                                                 ps[:, 0:3, :], ACT.Copy).then_inc(f["ev_act"][0], 1)
                for k in range(0, KD, 2):
                    act.wait_ge(*at(f["kT_done"], k + 1))
                    nc.scalar.activation(kT[:, k, :], ps[:, k, 0:T], ACT.Copy).then_inc(f["kT_a"][0], 1)
                act.wait_ge(*at(f["zma"], 2))
                nc.scalar.activation(za[:, :, :], za[:, :, :], ACT.Exp, scale=-1.0).then_inc(f["ze"][0], 1)
                act.wait_ge(*at(f["ze"], 1))
                nc.scalar.activation(z[:, :, :], za[:, :, :], ACT.Ln, bias=1.0).then_inc(f["zl"][0], 1)
                with act.Fori(0, 4) as it:
                    for s in range(4):
                        act.wait_ge(*at(f["nmax"], 4 * it + (s + 1)))
                        nc.scalar.activation(p_p[:, s, 0:P], ps[:, s, 0:P], ACT.Exp, bias=nmx[:, s, 0:1],
                                             scale=SCALE, accum_out=rs[:, s, 0:1])
                        nc.scalar.activation(p_p[:, s, P:T], ps[:, s, P:T], ACT.Exp, bias=nmx[:, s, 1:2],
                                             scale=SCALE, accum_out=rs[:, s, 1:2]).then_inc(f["exp"][0], 1)
                        if s >= 1:
                            prompt_pT(f, it, s - 1)
                    prompt_pT(f, it, 3)
                transposed(f["oT"], f["oT_32"], f["oT_lo"], width=SEQ)
                with act.Fori(0, 4) as it:
                    for t in range(4):
                        sample_k(f, it, t)
                        if t >= 1:
                            sample_exp(f, it, t - 1)
                            if t >= 2:
                                sample_o(f, it, t - 2)
                    sample_exp(f, it, 3)
                    sample_o(f, it, 2)
                    sample_o(f, it, 3)
                ahead(START[i]["out"])
                ahead(START[i]["out"] + CU)

            def prompt_pT(f, it, s):
                act.wait_ge(*at(f["pT"], 4 * it + (s + 1)))
                nc.scalar.activation(pT_p[:, s % 2, :], ps[:, 4 + s % 2, 0:T], ACT.Copy).then_inc(f["pT_ev"][0], 1)

            def sample_k(f, it, t):
                hf = t % 2
                act.wait_ge(*at(f["ktr"], 4 * it + (t + 1)))
                nc.scalar.activation(ktc[:, 4 * hf:4 * hf + 2, :], ps[:, 0, :].rearrange("p (g s) -> p g s", g=2),
                                     ACT.Copy).then_inc(f["kt_a"][0], 1)

            def sample_exp(f, it, t):
                hf, bank = t % 2, 2 + t % 2
                b16 = 32 * it + (16 * (t // 2) + PAST)
                act.wait_ge(*at(f["s_nmax"], 4 * it + (t + 1)))
                nc.scalar.activation(p_s[:, hf, 0:PAST], ps[:, bank, 0:PAST], ACT.Exp, bias=nmx[:, hf, 0:1],
                                     scale=SCALE, accum_out=rs[:, hf, 0:1])
                nc.scalar.activation(p_s[:, hf, ds(b16, DT)], ps[:, bank, PAST:PAST + DT], ACT.Exp,
                                     bias=nmx[:, hf, 0:1], scale=SCALE,
                                     accum_out=rs[:, hf, 1:2]).then_inc(f["s_exp"][0], 1)

            def sample_o(f, it, t):
                hf, bank = t % 2, 6 + t % 2
                b16 = 32 * it + (16 * (t // 2) + SEQ)
                act.wait_ge(*at(f["s_o"], 4 * it + (t + 1)))
                for e in range(2):
                    rows = slice(HD * e, HD * e + HD)
                    ins = nc.scalar.activation(
                        xT_hi[rows, 4 * hf:4 * hf + 4, ds(b16, DT)],
                        ps[rows, bank, 0:P].rearrange("p (g e q) -> p g e q", g=4, e=2)[:, :, e, :], ACT.Copy)
                ins.then_inc(f["s_o_hi"][0], 1)

            def hgrn(i, j):
                f, m0 = HGR[i], START[i]["mix"]
                for c in range(8):
                    ahead(m0 + CU * c)
                    act.wait_ge(unit_used, m0 + CU * (c + 1))
                    b0 = 4 * (c % 2)
                    h4 = slice(4 * (c % 2), 4 * (c % 2) + 4)
                    cols = slice(WCOLS * (c % 2), WCOLS * (c % 2) + WCOLS)
                    if c < 2:
                        if c == 0:
                            act.wait_ge(*at(LN[2 * i - 1]["x"], NTOK))
                        nc.scalar.activation(qT[:, h4, :], ps[:, b0:b0 + 4, 0:T], ACT.Silu).then_inc(f["ev"][0], 1)
                    elif c < 4:
                        nc.scalar.activation(sp[:, h4, :], ps[:, b0:b0 + 4, 0:T], ACT.Sigmoid)
                        nc.scalar.activation(sn[:, h4, :], ps[:, b0:b0 + 4, 0:T], ACT.Sigmoid,
                                             scale=-1.0).then_inc(f["ev"][0], 1)
                    elif c < 6:
                        nc.scalar.activation(vg[:, 0, :, cols], ps[:, b0:b0 + 3, :], ACT.Copy).then_inc(f["ev"][0], 1)
                    else:
                        nc.scalar.activation(vg[:, 1, :, cols], ps[:, b0:b0 + 3, :], ACT.Silu).then_inc(f["ev"][0], 1)
                act.wait_ge(*at(f["ev"], 8))

                def head(h2, s):
                    h = 2 * h2 + s
                    if not (iv(h2) and h2 == 0 and s == 0):
                        act.wait_ge(*at(f["o"], h))
                        act.wait_ge(*at(f["out"], h))
                    nc.scalar.activation(b_h[:, :], sp[:, ds(h, 1), :], ACT.Ln, bias=lb_col[:, ds(h, 1)],
                                         scale=oml_col[:, ds(h, 1)]).then_inc(f["g"][0], 1)
                    act.wait_ge(*at(f["b"], h + 1))
                    nc.scalar.activation(e_b[:, :], b_h[:, :], ACT.Exp).then_inc(f["expb"][0], 1)
                    act.wait_ge(*at(f["sub"], 8 * h + 8))
                    nc.scalar.activation(e_l[:, :], e_l[:, :], ACT.Exp).then_inc(f["expb"][0], 1)
                    nc.scalar.activation(lev[:, :], lev[:, :], ACT.Abs).then_inc(f["abs"][0], 1)
                    act.wait_ge(*at(f["abs"], h + 1))
                    nc.scalar.activation(lev[:, :], lev[:, :], ACT.Exp, scale=-1.0).then_inc(f["expl"][0], 1)
                    act.wait_ge(*at(f["k2T"], h + 1))
                    nc.scalar.activation(k2T[:, :], ps[:, 4, 0:T], ACT.Copy).then_inc(f["k2T_ev"][0], 1)
                    act.wait_ge(*at(f["o"], h + 1))
                    act.wait_ge(*at(f["sfin_ev"], h + 1))
                    for t in range(NTOK):
                        nc.scalar.activation(sq[:, :], ps[:, 5, t * P:(t + 1) * P], ACT.Square,
                                             accum_out=ss[:, t:t + 1]).then_inc(f["ss"][0], 1)
                        act.wait_ge(*at(f["ss"], NTOK * h + (t + 1)))

                head(0, 0)
                head(0, 1)
                with act.Fori(1, 4) as h2:
                    head(h2, 0)
                    head(h2, 1)
                transposed(f["oT"], f["oT_32"], f["oT_lo"])
                ahead(START[i]["out"])
                ahead(START[i]["out"] + CU)

            def pool(i, j):
                f = POOL[i]
                for k in range(KD):
                    act.wait_ge(*at(TR[2 * i]["done"], k + 1))
                    for dst, src in ((ext_p[:, k, HIST:], ps[:, k, 0:SEQ]),
                                     (ext_s[:, k, :, HIST:], ps[:, k, SEQ:T].rearrange("p (b t) -> p b t", b=DB))):
                        nc.scalar.activation(dst, src, ACT.Identity,
                                             bias=gbT[:, k, 2 * i + 2 * DEPTH - 1:2 * i + 2 * DEPTH],
                                             scale=gbT[:, k, 2 * i - 1:2 * i]).then_inc(f["ext"][0], 1)
                for k in range(KD):
                    act.wait_ge(*at(f["hist_T"], k + 1))
                    nc.scalar.activation(ext_s[:, k, :, 0:HIST],
                                         ps[:, k, 0:DB * HIST].rearrange("p (b r) -> p b r", b=DB),
                                         ACT.Copy).then_inc(f["hist_ev"][0], 1)
                for g in range(4):
                    act.wait_ge(*at(f["z"], g + 1))
                    nc.scalar.activation(xT_hi[:, 2 * g:2 * g + 2, :], zp[:, 2 * g:2 * g + 2, :],
                                         ACT.Copy).then_inc(f["hi"][0], 1)
                for u in range(2):
                    w_hi_of(START[i]["out"] + RING + u)

            for u in range(RING):
                w_hi_of(u)
            act.wait_ge(lb_steps, 2)
            nc.scalar.activation(lbT[:, :, :], lbT[:, :, :], ACT.Exp).then_inc(lb_steps, 1)
            def transposed_x(n):
                transposed(TR[n]["done"], TR[n]["t32"], TR[n]["lo"], n, affine=n > 0)

            transposed_x(0)
            for i in range(DEPTH):
                {"fox": fox, "hgrn": hgrn, "pool": pool}[KINDS[i % 3]](i, i // 3)
                transposed_x(2 * i + 1)
                if i % 3 == 0:
                    act.wait_ge(*at(FOX[i]["stored"], 16 * 6))
                elif i % 3 == 1:
                    for k in ("stored0", "stored1", "pstored0", "pstored1"):
                        act.wait_ge(*at(HGR[i][k], 16 * (HG // 2)))
                ffn(i)
                if i + 1 < DEPTH and KINDS[(i + 1) % 3] != "pool":
                    transposed_x(2 * i + 2)

        @block.vector
        def _(dve):
            V = nc.vector

            def w_lo_of(m, c=0):
                if iv(c) and m + CU * c >= UNITS:
                    return
                slot = m % RING
                dve.wait_ge(hi_ready, CU * c + (m + 1))
                V.tensor_tensor(w_lo[:, slot, :], w_raw[:, slot, :], w_hi[:, slot, :].bitcast(F32),
                                ALU.subtract).then_inc(lo_ready, 1)

            def ahead(m0, c=0):
                for u in range(CU):
                    w_lo_of(m0 + RING + u, c)

            def split(t32_at, hi, lo, width=T):
                for k in range(KD):
                    dve.wait_ge(*at(t32_at, k + 1))
                    V.tensor_copy(xT_hi[:, k, 0:width], t32[:, k % 2, 0:width]).then_inc(hi[0], 1)
                    dve.wait_ge(*at(hi, k + 1))
                    V.tensor_tensor(xT_lo[:, k, 0:width], t32[:, k % 2, 0:width], xT_hi[:, k, 0:width].bitcast(F32),
                                    ALU.subtract).then_inc(lo[0], 1)

            def split_x(n):
                split(TR[n]["t32"], TR[n]["hi"], TR[n]["lo"])

            def rsqrt(v, r, mark, before):
                dve.wait_ge(*at(mark, before + 1))
                V.tensor_scalar(r.bitcast(I32), v.bitcast(I32), 1, None, ALU.logical_shift_right).then_inc(mark[0], 1)
                dve.wait_ge(*at(mark, before + 2))
                V.tensor_scalar(r.bitcast(I32), r.bitcast(I32), -1.0, float(0x5F3759DF), ALU.mult,
                                ALU.add).then_inc(mark[0], 1)
                for n in range(NEWTON):
                    dve.wait_ge(*at(mark, before + 3 + 3 * n))
                    V.scalar_tensor_tensor(out=nt[:, :], in0=r, scalar=-0.5, in1=r, op0=ALU.mult,
                                           op1=ALU.mult).then_inc(mark[0], 1)
                    dve.wait_ge(*at(mark, before + 4 + 3 * n))
                    V.tensor_tensor(nt[:, :], nt[:, :], v, ALU.mult).then_inc(mark[0], 1)
                    dve.wait_ge(*at(mark, before + 5 + 3 * n))
                    V.scalar_tensor_tensor(out=r, in0=nt[:, :], scalar=1.5, in1=r, op0=ALU.add,
                                           op1=ALU.mult).then_inc(mark[0], 1)

            def layer_norm(n, done, sets, scaled=None):
                ln = LN[n]
                if n:
                    dve.wait_ge(*at(LN[n - 1]["x"], NTOK))
                for h in range(2):
                    cols = slice(h * WCOLS, (h + 1) * WCOLS)
                    dve.wait_ge(unit_used, done[h])
                    for t in range(NTOK):
                        y = ps[:, 4 * sets[h] + t, :]
                        if scaled is not None:
                            k = NTOK * h + t
                            if k >= 2:
                                dve.wait_ge(*at(ln["resid"], k - 1))
                            V.tensor_tensor(ysc[:, k % 2, :], y, scale_bc[:, cols], ALU.mult).then_inc(scaled[0], 1)
                            dve.wait_ge(*at(scaled, k + 1))
                            y = ysc[:, k % 2, :]
                        V.scalar_tensor_tensor(out=xn[:, t, cols], in0=x_tok[:, t, cols], scalar=ALPHA, in1=y,
                                               op0=ALU.mult, op1=ALU.add).then_inc(ln["resid"][0], 1)
                for t in range(NTOK):
                    dve.wait_ge(*at(ln["resid"], NTOK + t + 1))
                    for h in range(2):
                        ins = V.bn_stats(stats[:, t, h, :], xn[:, t, h * WCOLS:(h + 1) * WCOLS])
                    ins.then_inc(ln["stat"][0], 1)
                for t in range(NTOK):
                    dve.wait_ge(*at(ln["stat"], t + 1))
                    V.bn_aggr(mv[:, t, :], stats[:, t, :, :].rearrange("p a b -> p (a b)")).then_inc(ln["aggr"][0], 1)
                dve.wait_ge(*at(ln["aggr"], NTOK))
                V.tensor_scalar(var[:, :], mv[:, :, 1], LN_EPS, None, ALU.add).then_inc(ln["rstd"][0], 1)
                rsqrt(var[:, :], rstd[:, :], ln["rstd"], 0)
                for t in range(NTOK):
                    dve.wait_ge(*at(ln["rstd"], RSQRT))
                    V.tensor_scalar(xn[:, t, :], xn[:, t, :], mv[:, t, 0:1], rstd[:, t:t + 1], ALU.subtract,
                                    ALU.mult).then_inc(ln["xn"][0], 1)

            def ffn(i):
                f, m0 = FFN[i], START[i]["up"]

                def chunk(c, k):
                    ahead(m0, c)
                    dve.wait_ge(*at(f["silu"], c + 1))
                    if not (iv(c) and c < 2):
                        dve.wait_ge(*at(f["hi"], c - 1))
                        dve.wait_ge(*at(f["lo"], c - 1))
                    V.tensor_tensor(h32[:, k], sg[:, k], ps[:, 4 * k + 2:4 * k + 4, 0:T],
                                    ALU.mult).then_inc(f["h32"][0], 1)
                    dve.wait_ge(*at(f["hi"], c + 1))
                    V.tensor_tensor(hT_lo[:, ds(2 * c, 2), :], h32[:, k], hT_hi[:, ds(2 * c, 2), :].bitcast(F32),
                                    ALU.subtract).then_inc(f["lo"][0], 1)

                chunk(0, 0)
                chunk(1, 1)
                with dve.Fori(2, CF - 1, 2) as c:
                    chunk(c, 0)
                    chunk(c + 1, 1)
                chunk(CF - 1, 0)
                for u in range(2 * CF):
                    w_lo_of(START[i]["down"] + u + RING)

            def fox(i, j):
                f, m0 = FOX[i], START[i]["mix"]
                V.memset(ones[:, :], 1.0).then_inc(f["ones"][0], 1)
                ahead(m0)
                ahead(m0 + CU)
                dve.wait_ge(unit_used, m0 + 2 * CU)
                V.tensor_copy(qT[:, 4:8, :], ps[:, 4:8, 0:T]).then_inc(f["ev_dve"][0], 1)
                dve.wait_ge(*at(f["wf_hi"], 1))
                V.tensor_tensor(wf_lo[:, :, :], wf[:, :, :], wf_hi[:, :, :].bitcast(F32),
                                ALU.subtract).then_inc(f["wf_lo"][0], 1)
                with dve.Fori(0, 2) as w:
                    for h in range(2):
                        for u in range(CU):
                            w_lo_of(m0 + (2 + h) * CU + RING + u, 2 * w)
                    dve.wait_ge(unit_used, 2 * CU * w + (m0 + 4 * CU))
                    V.tensor_copy(kv_tok[:, ds(w, 1), :, WCOLS:D], ps[:, 4:7, :]).then_inc(f["ev_dve"][0], 1)
                dve.wait_ge(*at(f["fproj"], 1))
                dve.wait_ge(*at(f["bf_in"], 16))
                V.tensor_tensor(z[:, :, :], ps[:, 7, 0:NTOK * HEADS].rearrange("p (t h) -> p t h", t=NTOK),
                                bf[:, :].unsqueeze(1).broadcast_to([P, NTOK, HEADS]), ALU.add).then_inc(f["z"][0], 1)
                dve.wait_ge(*at(f["z"], 1))
                V.tensor_scalar(zm[:, :, :], z[:, :, :], 0.0, None, ALU.min).then_inc(f["zma"][0], 1)
                V.scalar_tensor_tensor(out=za[:, :, :], in0=z[:, :, :], scalar=-1.0, in1=z[:, :, :], op0=ALU.mult,
                                       op1=ALU.max).then_inc(f["zma"][0], 1)
                dve.wait_ge(*at(f["zl"], 1))
                V.tensor_tensor(lf_tok[:, :, :], zm[:, :, :], z[:, :, :], ALU.subtract).then_inc(f["lf"][0], 1)
                for k in range(1, KD, 2):
                    dve.wait_ge(*at(f["kT_done"], k + 1))
                    V.tensor_copy(kT[:, k, :], ps[:, k, 0:T]).then_inc(f["kT_d"][0], 1)
                for hf in range(2):
                    ins = V.tensor_copy(heads8[:, hf, :].rearrange("p (h q) -> p h q", q=DT),
                                        ident[0:HEADS, 8 * hf:8 * hf + 8].unsqueeze(2).broadcast_to([HEADS, 8, DT]))
                ins.then_inc(f["heads8"][0], 1)
                dve.wait_ge(*at(f["lfT_done"], 1))
                V.tensor_scalar(cp[:, :], ps[0:HEADS, 0, 0:SEQ], -1.0 / SCALE, None, ALU.mult).then_inc(f["c_raw"][0], 1)
                V.tensor_scalar(craw[:, :, PAST:], ps[0:HEADS, 0, SEQ:T].rearrange("p (b t) -> p b t", b=DB),
                                -1.0 / SCALE, None, ALU.mult).then_inc(f["c_raw"][0], 1)
                V.tensor_scalar(craw[:, :, 0:PAST], ps[0:HEADS, 4:8, :].rearrange("p a (b t) -> p (a b) t", b=2),
                                -1.0 / SCALE, None, ALU.mult).then_inc(f["c_raw"][0], 1)
                dve.wait_ge(*at(f["c_raw"], 3))
                dve.wait_ge(*at(f["ones"], 1))
                V.tensor_tensor_scan(cp[:, :], ones[:, 0:SEQ], cp[:, :], 0.0, ALU.mult, ALU.add).then_inc(f["c"][0], 1)
                for b in range(DB):
                    V.tensor_tensor_scan(craw[:, b, :], ones[:, :], craw[:, b, :], 0.0, ALU.mult,
                                         ALU.add).then_inc(f["c"][0], 1)

                dve.wait_ge(*at(f["stored"], 16 * 6))

                def prompt_max(it, s):
                    dve.wait_ge(*at(f["scores"], 4 * it + (s + 1)))
                    V.tensor_reduce(mx[:, s, 0:1], ps[:, s, 0:P], AX_X, ALU.max)
                    V.tensor_reduce(mx[:, s, 1:2], ps[:, s, P:T], AX_X, ALU.max).then_inc(f["max"][0], 1)
                    dve.wait_ge(*at(f["max"], 4 * it + (s + 1)))
                    V.tensor_scalar(nmx[:, s, :], mx[:, s, :], -SCALE, None, ALU.mult).then_inc(f["nmax"][0], 1)

                def prompt_out(it, s):
                    dve.wait_ge(*at(f["exp"], 4 * it + (s + 1)))
                    V.reciprocal(rcp[:, s, :], rs[:, s, :]).then_inc(f["rcp"][0], 1)
                    dve.wait_ge(*at(f["rcp"], 4 * it + (s + 1)))
                    dve.wait_ge(*at(f["o"], 4 * it + (s + 1)))
                    for q in range(2):
                        ins = V.tensor_scalar(o_tok[:, q, ds(4 * HD * it + HD * s, HD)],
                                              ps[:, 6 + s % 2, q * HD:(q + 1) * HD],
                                              rcp[:, s, q:q + 1], None, ALU.mult)
                    ins.then_inc(f["o_ev"][0], 1)

                with dve.Fori(0, 4) as it:
                    for s in range(4):
                        prompt_max(it, s)
                        if s >= 2:
                            prompt_out(it, s - 2)
                    prompt_out(it, 2)
                    prompt_out(it, 3)
                split(f["oT_32"], f["oT_hi"], f["oT_lo"], SEQ)

                def sample_k(it, t):
                    hf = t % 2
                    dve.wait_ge(*at(f["ktr"], 4 * it + (t + 1)))
                    V.tensor_copy(ktc[:, 4 * hf + 2:4 * hf + 4, :],
                                  ps[:, 1, :].rearrange("p (g s) -> p g s", g=2)).then_inc(f["kt_d"][0], 1)

                def sample_max(it, t):
                    hf = t % 2
                    dve.wait_ge(*at(f["s_scores"], 4 * it + (t + 1)))
                    V.memset(p_s[:, hf, PAST:T], 0.0)
                    V.tensor_reduce(mx[:, hf, 0:1], ps[:, 2 + hf, 0:PAST + DT], AX_X, ALU.max).then_inc(f["s_max"][0], 1)
                    dve.wait_ge(*at(f["s_max"], 4 * it + (t + 1)))
                    V.tensor_scalar(nmx[:, hf, 0:1], mx[:, hf, 0:1], -SCALE, None, ALU.mult).then_inc(f["s_nmax"][0], 1)

                def sample_p(it, t):
                    hf = t % 2
                    dve.wait_ge(*at(f["s_exp"], 4 * it + (t + 1)))
                    V.tensor_tensor(rt[:, hf:hf + 1], rs[:, hf, 0:1], rs[:, hf, 1:2], ALU.add).then_inc(f["s_sum"][0], 1)
                    dve.wait_ge(*at(f["s_sum"], 4 * it + (t + 1)))
                    V.reciprocal(rcp[:, hf, 0:1], rt[:, hf:hf + 1]).then_inc(f["s_rcp"][0], 1)
                    dve.wait_ge(*at(f["s_rcp"], 4 * it + (t + 1)))
                    V.tensor_scalar(p_s[:, hf, :], p_s[:, hf, :], rcp[:, hf, 0:1], None,
                                    ALU.mult).then_inc(f["s_p"][0], 1)

                def sample_pT(it, t):
                    hf = t % 2
                    dve.wait_ge(*at(f["s_pT"], 4 * it + (t + 1)))
                    V.tensor_copy(pT_s[:, hf, :], ps[:, 4 + hf, 0:T]).then_inc(f["s_pT_ev"][0], 1)

                def sample_o(it, t):
                    hf = t % 2
                    b16 = 32 * it + (16 * (t // 2) + SEQ)
                    dve.wait_ge(*at(f["s_o_hi"], 4 * it + (t + 1)))
                    for e in range(2):
                        rows = slice(HD * e, HD * e + HD)
                        dst = (slice(4 * hf, 4 * hf + 4), ds(b16, DT))
                        ins = V.tensor_tensor(
                            xT_lo[rows, dst[0], dst[1]],
                            ps[rows, 6 + hf, 0:P].rearrange("p (g e q) -> p g e q", g=4, e=2)[:, :, e, :],
                            xT_hi[rows, dst[0], dst[1]].bitcast(F32), ALU.subtract)
                    ins.then_inc(f["s_o_lo"][0], 1)

                with dve.Fori(0, 4) as it:
                    for t in range(4):
                        sample_k(it, t)
                        sample_max(it, t)
                        if t >= 1:
                            sample_pT(it, t - 1)
                        sample_p(it, t)
                        if t >= 1:
                            sample_o(it, t - 1)
                    sample_pT(it, 3)
                    sample_o(it, 3)
                ahead(START[i]["out"])
                ahead(START[i]["out"] + CU)

            def hgrn(i, j):
                f, m0 = HGR[i], START[i]["mix"]
                V.memset(cut[:, :], 1.0).then_inc(f["consts"][0], 1)
                V.memset(q_blk[:, :, :], 0.0)
                dve.wait_ge(*at(f["consts"], 1))
                V.memset(cut[:, 0:SEQ:P], 0.0)
                V.memset(cut[:, SEQ:T:DT], 0.0).then_inc(f["consts"][0], 1)
                for c in range(8):
                    ahead(m0 + CU * c)
                dve.wait_ge(*at(f["ev"], 8))
                dve.wait_ge(*at(f["consts"], 2))
                dve.wait_ge(*at(f["pconst"], 3))

                def head(h2, s):
                    h = 2 * h2 + s
                    if not (iv(h2) and h2 == 0 and s == 0):
                        dve.wait_ge(*at(f["o"], h))
                        dve.wait_ge(*at(f["upd"], h))
                    V.tensor_scalar(k_h[:, :], sn[:, ds(h, 1), :], oml_col[:, ds(h, 1)], None,
                                    ALU.mult).then_inc(f["k"][0], 1)
                    dve.wait_ge(*at(f["g"], h + 1))
                    V.tensor_tensor_scan(b_h[:, :], cut[:, :], b_h[:, :], 0.0, ALU.mult, ALU.add).then_inc(f["b"][0], 1)
                    dve.wait_ge(*at(f["b"], h + 1))
                    for m, off, n in zip(LEVELS, LOFF, LCOLS):
                        blk = b_h[:, 0:n].rearrange("p (a m) -> p a m", m=2 * m)
                        V.tensor_tensor(lev[:, off:off + n].rearrange("p (a m) -> p a m", m=2 * m), blk,
                                        blk[:, :, m - 1:m].broadcast_to([P, n // (2 * m), 2 * m]),
                                        ALU.subtract).then_inc(f["sub"][0], 1)
                    for lo, hi, m in ((0, SEQ, P), (SEQ, T, DT)):
                        blk = b_h[:, lo:hi].rearrange("p (a m) -> p a m", m=m)
                        ins = V.tensor_tensor(e_l[:, lo:hi].rearrange("p (a m) -> p a m", m=m),
                                              blk[:, :, m - 1:m].broadcast_to([P, (hi - lo) // m, m]), blk, ALU.subtract)
                    ins.then_inc(f["sub"][0], 1)
                    dve.wait_ge(*at(f["expb"], 2 * h + 2))
                    dve.wait_ge(*at(f["k"], h + 1))
                    V.tensor_tensor(k2[:, :], k_h[:, :], e_l[:, :], ALU.mult).then_inc(f["k2"][0], 1)
                    V.tensor_tensor(q_e[:, :], qT[:, ds(h, 1), :], e_b[:, :].unsqueeze(1), ALU.mult).then_inc(f["qe"][0], 1)
                    dve.wait_ge(*at(f["qe"], h + 1))
                    diag = q_blk[:, :, :].rearrange("p b t -> p (b t)")
                    for b in range(DB):
                        ins = V.tensor_copy(q_blk[:, b, DT * b:DT * b + DT], q_e[:, SEQ + DT * b:SEQ + DT * b + DT])
                    ins.then_inc(f["qb"][0], 1)
                    dve.wait_ge(*at(f["expl"], h + 1))
                    for m, off, n in zip(LEVELS, LOFF, LCOLS):
                        w = lev[:, off:off + n].rearrange("p (a e m) -> p a e m", e=2, m=m)
                        qv = qT[:, ds(h, 1), 0:n].rearrange("p o (a e m) -> p (o a) e m", e=2, m=m)
                        kv = k_h[:, 0:n].rearrange("p (a e m) -> p a e m", e=2, m=m)
                        V.tensor_tensor(w[:, :, 0, :], w[:, :, 0, :], kv[:, :, 0, :], ALU.mult)
                        ins = V.tensor_tensor(w[:, :, 1, :], w[:, :, 1, :], qv[:, :, 1, :], ALU.mult)
                    ins.then_inc(f["lq"][0], 1)
                    for t in range(NTOK):
                        n = TILE_LEVELS[t] + 1
                        dve.wait_ge(*at(f["sc"], NTOK * h + (t + 1)))
                        bank = 2 * (t % 2)
                        nn = [(0, 4), (4, n)] if n > 4 else [(0, n)]
                        for a, (lo, hi) in enumerate(nn):
                            ins = V.tensor_tensor(sc[:, t % 2, lo:hi, :],
                                                  ps[:, bank + a, 0:(hi - lo) * P].rearrange("p (l s) -> p l s", s=P),
                                                  lmask[:, lo:hi, :], ALU.mult)
                        ins.then_inc(f["scm"][0], 1)
                    dve.wait_ge(*at(f["s1"], h + 1))
                    V.tensor_copy(s1[:, :], ps[:, 4, T:T + P]).then_inc(f["s1_ev"][0], 1)
                    dve.wait_ge(*at(f["s1_ev"], h + 1))
                    dve.wait_ge(*at(f["sfin"], h + 1))
                    if not (iv(h2) and h2 == 0):
                        dve.wait_ge(*at(f[f"pstored{s}"], 16 * h2))
                    V.scalar_tensor_tensor(out=s_fin[:, s, :], in0=s1[:, :], scalar=e_b[:, SEQ - 1:SEQ],
                                           in1=ps[:, 5, T:T + P], op0=ALU.mult, op1=ALU.add).then_inc(f["sfin_ev"][0], 1)
                    dve.wait_ge(*at(f["upd"], h + 1))
                    for b in range(DB):
                        ins = V.scalar_tensor_tensor(
                            out=S_b[:, s, b, :], in0=S_b[:, s, b, :], scalar=e_b[:, SEQ + DT * b + DT - 1:SEQ + DT * b + DT],
                            in1=ps[:, 6 + b // 4, (b % 4) * P:(b % 4 + 1) * P], op0=ALU.mult, op1=ALU.add)
                    ins.then_inc(f["snew"][0], 1)
                    dve.wait_ge(*at(f["ss"], NTOK * h + NTOK))
                    V.tensor_scalar(var[:, :], ss[:, :], 1.0 / P, RMS_EPS, ALU.mult, ALU.add).then_inc(f["rr"][0], 1)
                    rsqrt(var[:, :], rr[:, :], f["rr"], RSQRT * h)
                    dve.wait_ge(*at(f["rr"], RSQRT * h + RSQRT))
                    dve.wait_ge(*at(f["gate"], 1))
                    dve.wait_ge(*at(f["vm"], h + 1))
                    for t in range(NTOK):
                        ins = V.scalar_tensor_tensor(out=vg[:, 0, t, ds(P * h, P)], in0=ps[:, 5, t * P:(t + 1) * P],
                                                     scalar=rr[:, t:t + 1], in1=vg[:, 1, t, ds(P * h, P)],
                                                     op0=ALU.mult, op1=ALU.mult)
                    ins.then_inc(f["out"][0], 1)

                head(0, 0)
                head(0, 1)
                with dve.Fori(1, 4) as h2:
                    head(h2, 0)
                    head(h2, 1)
                split(f["oT_32"], f["oT_hi"], f["oT_lo"])
                ahead(START[i]["out"])
                ahead(START[i]["out"] + CU)

            def pool(i, j):
                f = POOL[i]
                V.memset(ext_p[:, :, 0:HIST], 0.0).then_inc(f["w"][0], 1)
                dve.wait_ge(*at(f["ext"], 2 * KD))
                dve.wait_ge(*at(f["hist_ev"], KD))
                dve.wait_ge(*at(f["consts"], 2))
                step = 1

                def chained(ins):
                    nonlocal step
                    ins.then_inc(f["w"][0], 1)
                    step += 1

                chained(V.reciprocal(cnt[:, :], cnt[:, :]))
                for g in range(4):
                    k2s = slice(2 * g, 2 * g + 2)
                    pp, sss = ext_p[:, k2s, :], ext_s[:, k2s, :, :]
                    for e in range(g + 1):
                        d, lo = 1 << e, (1 << (e + 1)) - 1
                        dve.wait_ge(*at(f["w"], step))
                        po, so = wp[e % 2], ws[e % 2]
                        chained(V.tensor_tensor(po[:, :, lo:], pp[:, :, lo:], pp[:, :, lo - d:HIST + SEQ - d], ALU.add))
                        for kk in range(2):
                            chained(V.tensor_tensor(so[:, kk, :, lo:], sss[:, kk, :, lo:],
                                                    sss[:, kk, :, lo - d:HIST + DT - d], ALU.add))
                        pp, sss = po[:, :, :], so[:, :, :, :]
                    dve.wait_ge(*at(f["w"], step))
                    w = 2 << g
                    chained(V.scalar_tensor_tensor(out=zp[:, k2s, 0:SEQ], in0=pp[:, :, HIST:], scalar=1.0 / w,
                                                   in1=ext_p[:, k2s, HIST:], op0=ALU.mult, op1=ALU.subtract))
                    chained(V.tensor_tensor(zq[:, :, 0:w], pp[:, :, HIST:HIST + w],
                                            cnt[:, 0:w].unsqueeze(1).broadcast_to([P, 2, w]), ALU.mult))
                    dve.wait_ge(*at(f["w"], step))
                    chained(V.tensor_tensor(zp[:, k2s, 0:w], zq[:, :, 0:w], ext_p[:, k2s, HIST:HIST + w], ALU.subtract))
                    for kk in range(2):
                        ins = V.scalar_tensor_tensor(
                            out=zp[:, 2 * g + kk, SEQ:T].rearrange("p (b t) -> p b t", b=DB), in0=sss[:, kk, :, HIST:],
                            scalar=1.0 / w, in1=ext_s[:, 2 * g + kk, :, HIST:], op0=ALU.mult, op1=ALU.subtract)
                        chained(ins)
                    dve.wait_ge(*at(f["w"], step))
                    V.tensor_copy(mv[:, 0, :], mv[:, 0, :]).then_inc(f["z"][0], 1)
                for g in range(4):
                    dve.wait_ge(*at(f["hi"], g + 1))
                    V.tensor_tensor(xT_lo[:, 2 * g:2 * g + 2, :], zp[:, 2 * g:2 * g + 2, :],
                                    xT_hi[:, 2 * g:2 * g + 2, :].bitcast(F32), ALU.subtract).then_inc(f["lo"][0], 1)
                for u in range(2):
                    w_lo_of(START[i]["out"] + RING + u)

            V.memset(mv[:, :, :], 0.0)
            for u in range(RING):
                w_lo_of(u)
            dve.wait_ge(rowsT_done, 1)
            V.tensor_copy(gbT[:, :, :], ps[:, 6, 0:KD * 4 * DEPTH].rearrange("p (k r) -> p k r", k=KD)).then_inc(gbT_ready, 1)
            V.tensor_copy(lbT[:, :, :], ps[:, 7, 0:KD * DEPTH].rearrange("p (k r) -> p k r", k=KD)).then_inc(gbT_ready, 1)
            dve.wait_ge(gbT_ready, 2)
            V.tensor_reduce(lb_max[:, :], lbT[:, :, :], AX_X, ALU.max).then_inc(lb_steps, 1)
            dve.wait_ge(lb_steps, 1)
            V.tensor_tensor(lbT[:, :, :], lbT[:, :, :], lb_max[:, :].unsqueeze(2).broadcast_to([P, KD, DEPTH]),
                            ALU.subtract).then_inc(lb_steps, 1)
            dve.wait_ge(lb_steps, 3)
            V.tensor_reduce(lb_sum[:, :], lbT[:, :, :], AX_X, ALU.add).then_inc(lb_steps, 1)
            dve.wait_ge(lb_steps, 4)
            V.reciprocal(lb_sum[:, :], lb_sum[:, :]).then_inc(lb_steps, 1)
            dve.wait_ge(lb_steps, 5)
            V.tensor_tensor(lb_col[:, :], lbT[:, :, 1], lb_sum[:, :], ALU.mult).then_inc(lb_steps, 1)
            dve.wait_ge(lb_steps, 6)
            V.tensor_scalar(oml_col[:, :], lb_col[:, :], -1.0, 1.0, ALU.mult, ALU.add).then_inc(lb_steps, 1)
            split_x(0)
            for i in range(DEPTH):
                s = START[i]
                kind = KINDS[i % 3]
                {"fox": fox, "hgrn": hgrn, "pool": pool}[kind](i, i // 3)
                if kind == "pool":
                    dve.wait_ge(*at(POOL[i]["consts"], 2))
                    dve.wait_ge(*at(POOL[i]["in"], 32))
                    layer_norm(2 * i, (s["out"] + 1, s["out"] + 2), (0, 1), POOL[i]["ysc"])
                else:
                    layer_norm(2 * i, (s["out"] + CU, s["out"] + 2 * CU), (0, 1))
                split_x(2 * i + 1)
                ffn(i)
                layer_norm(2 * i + 1, (s["down"] + CF, s["down"] + 2 * CF), (1, 0))
                if i + 1 < DEPTH and KINDS[(i + 1) % 3] != "pool":
                    split_x(2 * i + 2)

        @block.gpsimd
        def _(pool):
            G = nc.gpsimd

            def lone_wait():
                pool.wait_ge(rowsT_done, 1)

            def load_gb(n):
                pool.dma_start(gb[:, 0, :], ln_g[n // 2, n % 2, :].partition_broadcast(P)).then_inc(gb_loaded, 16)
                pool.dma_start(gb[:, 1, :], ln_b[n // 2, n % 2, :].partition_broadcast(P)).then_inc(gb_loaded, 16)

            def residual(n):
                ln = LN[n]
                pool.wait_ge(gb_loaded, 32 * (n + 1))
                for t in range(NTOK):
                    pool.wait_ge(*at(ln["xn"], t + 1))
                    G.tensor_tensor(x_tok[:, t, :], xn[:, t, :], gb[:, 0, :], ALU.mult).then_inc(ln["gx"][0], 1)
                    pool.wait_ge(*at(ln["gx"], t + 1))
                    G.tensor_tensor(x_tok[:, t, :], x_tok[:, t, :], gb[:, 1, :], ALU.add).then_inc(ln["x"][0], 1)
                pool.wait_ge(*at(ln["x"], NTOK))
                if n < LN_LAST:
                    load_gb(n + 1)

            def fox(i, j):
                f, m0 = FOX[i], START[i]["mix"]
                if i:
                    pool.wait_ge(unit_used, m0)
                pool.dma_start(wf[:, :, :], w_fox_in[j][:, 3 * D:].rearrange("(k p) h -> p k h", p=P)).then_inc(f["wf_in"][0], 16)
                pool.dma_start(bf[:, :], b_fox_f[j].partition_broadcast(P)).then_inc(f["bf_in"][0], 16)
                pool.dma_start(lfc[:, :, :], cache_fox_lf[j].rearrange("b (a p) h -> p (b a) h", p=P)).then_inc(f["lfc_in"][0], 16)

                def load_cache(b, s):
                    lone_wait()
                    for dst, src in ((k_c[s], cache_fox_k), (v_c[s], cache_fox_v)):
                        pool.dma_start(dst[:, :, :].unsqueeze(1),
                                       src[j][ds(b, 1)].rearrange("o (a p) h d -> p o a (h d)", p=P)).then_inc(
                                           f[f"kv{s}"][0], 16)

                load_cache(0, 0)
                pool.wait_ge(*at(f["ev_act"], 3))
                pool.wait_ge(*at(f["ev_dve"], 3))
                for n, (kp, ks) in enumerate(((fox_k_prompt, fox_k_sample), (fox_v_prompt, fox_v_sample))):
                    pool.dma_start(kp[j].rearrange("b (a p) h d -> p (b a) (h d)", p=P),
                                   kv_tok[:, n, 0:2, :]).then_inc(f["stored"][0], 16)
                    pool.dma_start(ks[j].rearrange("b t h d -> (b t) (h d)"), kv_tok[:, n, 2, :]).then_inc(f["stored"][0], 16)
                def stage(it, s):
                    G.tensor_copy(sel[:, s, :], ident[0:HEADS, ds(4 * it + s, 1)].broadcast_to([HEADS, P]))
                    G.tensor_tensor(q_s[:, s:s + 1, :], qT[:, ds(2 * it + s // 2, 1), 0:SEQ],
                                    half[:, s % 2:s % 2 + 1].unsqueeze(2).broadcast_to([P, 1, SEQ]),
                                    ALU.mult).then_inc(f["staged"][0], 1)

                for s in range(4):
                    stage(0, s)
                pool.wait_ge(*at(f["lf"], 1))
                pool.dma_start(fox_lf_prompt[j].rearrange("b (a p) h -> p (b a) h", p=P), lf_tok[:, 0:2, :]).then_inc(
                    f["stored"][0], 16)
                pool.dma_start(fox_lf_sample[j].rearrange("b t h -> (b t) h"), lf_tok[:, 2, :]).then_inc(f["stored"][0], 16)
                with pool.Fori(1, 4) as it:
                    for s in range(4):
                        pool.wait_ge(*at(f["scores"], 4 * it + (s - 3)))
                        stage(it, s)

                def stage_q(b, s):
                    cols = ds(DT * b + SEQ, DT)
                    G.tensor_copy(k_new[:, s, :, :], kT[:, :, cols])
                    for e in range(2):
                        ins = G.tensor_tensor(qbd[:, s, :, e, :], qT[:, :, cols],
                                              half[:, e:e + 1].unsqueeze(2).broadcast_to([P, KD, DT]), ALU.mult)
                    ins.then_inc(f["qst"][0], 1)

                stage_q(0, 0)
                stage_q(1, 1)
                pool.wait_ge(*at(f["oT_lo"], KD))
                load_cache(1, 1)
                with pool.Fori(0, 3) as it:
                    for s in range(2):
                        pool.wait_ge(*at(f["s_scores"], 4 * it + (2 * s + 2)))
                        stage_q(2 * it + (s + 2), s)
                        pool.wait_ge(*at(f["s_o"], 4 * it + (2 * s + 2)))
                        load_cache(2 * it + (s + 2), s)

            def hgrn(i, j):
                f, m0 = HGR[i], START[i]["mix"]
                pool.wait_ge(unit_used, m0)
                pool.dma_start(ng[:, :], hgrn_norm_g[j].partition_broadcast(P)).then_inc(f["ng_in"][0], 16)

                def load_state(h, s):
                    lone_wait()
                    pool.dma_start(S_b[:, s, :, :].unsqueeze(1),
                                   state_hgrn[j][:, ds(h, 1)].rearrange("b o c v -> c o b v")).then_inc(
                                       f[f"st{s}_in"][0], 16)

                load_state(0, 0)
                load_state(1, 1)
                G.memset(lmask[:, :, :], 1.0).then_inc(f["pconst"][0], 1)
                G.memset(row_m[:, :], 1.0).then_inc(f["pconst"][0], 1)
                pool.wait_ge(*at(f["pconst"], 2))
                k = 0

                def select(view, pattern, base, mult):
                    nonlocal k
                    if k:
                        pool.wait_ge(*at(f["masks"], k))
                    G.affine_select(out=view, in_=view, pattern=pattern, compare_op=ALU.is_ge, fill=0.0, base=base,
                                    channel_multiplier=mult).then_inc(f["masks"][0], 1)
                    k += 1

                select(row_m[:, :], [[-DT, DB]], 0, 1)
                select(row_m[:, :], [[DT, DB]], DT - 1, -1)
                select(lmask[:, 0, :], [[1, P]], 0, -1)
                select(lmask[:, 0, :], [[-1, P]], 0, 1)
                for n, m in enumerate(LEVELS):
                    view = lmask[:, n + 1, :].rearrange("p (a r) -> p a r", r=2 * m)
                    na = P // (2 * m)
                    select(view, [[0, na], [1, 2 * m]], -m, 0)
                    select(view, [[-2 * m, na], [0, 2 * m]], 0, 1)
                    select(view, [[2 * m, na], [0, 2 * m]], m - 1, -1)
                pool.wait_ge(*at(f["masks"], k))
                G.memset(sq[:, :], 0.0).then_inc(f["pconst"][0], 1)
                pool.wait_ge(*at(f["ng_in"], 16))
                pool.wait_ge(*at(f["ev"], 8))
                for t in range(NTOK):
                    v = vg[:, 1, t, :].rearrange("p (h v) -> p h v", h=HG)
                    ins = G.tensor_tensor(v, v, ng[:, :].unsqueeze(1).broadcast_to([P, HG, P]), ALU.mult)
                ins.then_inc(f["gate"][0], 1)

                def head(h2, s):
                    h = 2 * h2 + s
                    if not (iv(h2) and h2 == 0 and s == 0):
                        pool.wait_ge(*at(f["upd"], h))
                    pool.wait_ge(*at(f["g"], h + 1))
                    G.tensor_tensor(v_m[:, :, :], vg[:, 0, 2, ds(P * h, P)].unsqueeze(1).broadcast_to([P, DB, P]),
                                    row_m[:, :].unsqueeze(2).broadcast_to([P, DB, P]), ALU.mult).then_inc(f["vm"][0], 1)
                    lone_wait()
                    pool.wait_ge(*at(f["sfin_ev"], h + 1))
                    pool.dma_start(hgrn_state_prompt[j, 0, ds(h, 1)].rearrange("o c v -> c o v"),
                                   s_fin[:, s:s + 1, :]).then_inc(f[f"pstored{s}"][0], 16)
                    lone_wait()
                    pool.wait_ge(*at(f["snew"], h + 1))
                    pool.dma_start(hgrn_state_sample[j][:, ds(h, 1)].rearrange("b o c v -> c o b v"),
                                   S_b[:, s, :, :].unsqueeze(1)).then_inc(f[f"stored{s}"][0], 16)

                head(0, 0)
                head(0, 1)
                with pool.Fori(1, 4) as h2:
                    for s in range(2):
                        pool.wait_ge(*at(f[f"stored{s}"], 16 * h2))
                        load_state(2 * h2 + s, s)
                        head(h2, s)

            def pooling(i, j):
                f = POOL[i]
                pool.wait_ge(unit_used, START[i]["out"])
                pool.dma_start(hist[:, :], cache_pool[j].rearrange("b r d -> (b r) d")).then_inc(f["in"][0], 16)
                pool.dma_start(scale_bc[:, :], pool_scale[j].partition_broadcast(P)).then_inc(f["in"][0], 16)
                G.iota(cnt[:, :], [[1, DT]], base=1, channel_multiplier=0,
                       allow_small_or_imprecise_dtypes=True).then_inc(f["consts"][0], 2)
                pool.dma_start(pool_prompt[j, 0], x_tok[P - HIST:P, 1, :]).then_inc(f["stored"][0], 16)
                for b in range(DB):
                    pool.dma_start(pool_sample[j, b], x_tok[DT * b + 1:DT * b + DT, 2, :]).then_inc(f["stored"][0], 16)
                pool.wait_ge(*at(f["stored"], 16 * (DB + 1)))

            pool.dma_start(x_tok[:, 0:2, :], x_prompt.rearrange("b (a p) d -> p (b a) d", p=P)).then_inc(x_loaded, 16)
            pool.dma_start(x_tok[:, 2, :], x_sample.rearrange("b t d -> (b t) d")).then_inc(x_loaded, 16)
            pool.dma_start(gb_rows[0:2 * DEPTH, :], ln_g.rearrange("i s d -> (i s) d")).then_inc(rows_loaded, 16)
            pool.dma_start(gb_rows[2 * DEPTH:4 * DEPTH, :], ln_b.rearrange("i s d -> (i s) d")).then_inc(rows_loaded, 16)
            pool.dma_start(lb_rows[:, :], hgrn_lb).then_inc(rows_loaded, 16)
            load_gb(0)
            G.memset(ident[:, :], 0.0).then_inc(const_set, 1)
            G.memset(causal[:, :], 0.0).then_inc(const_set, 1)
            G.memset(new_mask[:, :], 0.0).then_inc(const_set, 1)
            G.memset(half[:, :], 1.0).then_inc(const_set, 1)
            pool.wait_ge(const_set, 4)
            G.affine_select(out=ident[:, :], in_=ident[:, :], compare_op=ALU.not_equal, fill=1.0, base=0,
                            pattern=[[-1, P]], channel_multiplier=1).then_inc(ident_ready, 1)
            G.affine_select(out=causal[:, :], in_=causal[:, :], compare_op=ALU.is_ge, fill=MASKED, base=0,
                            pattern=[[-1, P]], channel_multiplier=1).then_inc(ident_ready, 1)
            G.affine_select(out=half[:, 0:1], in_=half[:, 0:1], compare_op=ALU.is_ge, fill=0.0, base=HD - 1,
                            pattern=[[0, 1]], channel_multiplier=-1).then_inc(ident_ready, 1)
            G.affine_select(out=half[:, 1:2], in_=half[:, 1:2], compare_op=ALU.is_ge, fill=0.0, base=-HD,
                            pattern=[[0, 1]], channel_multiplier=1).then_inc(ident_ready, 1)
            pool.wait_ge(ident_ready, 4)
            for h in range(KD):
                pool.dma_start(new_mask[DT * h:DT * h + DT, :], causal[0:DT, 0:DT]).then_inc(mask_loaded, 16)
            pool.wait_ge(rowsT_done, 1)
            for i in range(DEPTH):
                {"fox": fox, "hgrn": hgrn, "pool": pooling}[KINDS[i % 3]](i, i // 3)
                residual(2 * i)
                residual(2 * i + 1)
            pool.dma_start(y_prompt.rearrange("b (a p) d -> p (b a) d", p=P), x_tok[:, 0:2, :]).then_inc(y_stored, 16)
            pool.dma_start(y_sample.rearrange("b t d -> (b t) d"), x_tok[:, 2, :]).then_inc(y_stored, 16)
            pool.wait_ge(y_stored, 32)
            for i in FOX:
                pool.wait_ge(*at(FOX[i]["stored"], 16 * 6))
            for i in HGR:
                for k in ("stored0", "stored1", "pstored0", "pstored1"):
                    pool.wait_ge(*at(HGR[i][k], 16 * (HG // 2)))
            for i in POOL:
                pool.wait_ge(*at(POOL[i]["stored"], 16 * (DB + 1)))

        @block.tensor
        def _(pe):
            mm = nc.tensor.matmul

            def unit_fm(m, c, u, bank0, x_hi, x_lo, wait_x=None):
                slot = m % RING
                pe.wait_ge(lo_ready, CU * c + (m + 1))
                for kk in range(2):
                    k = 2 * u + kk
                    if wait_x is not None:
                        wait_x(k)
                    for n in range(4):
                        cols = slice(kk * WCOLS + n * P, kk * WCOLS + (n + 1) * P)
                        out = ps[:, bank0 + n, 0:T]
                        mm(out, w_hi[:, slot, cols], x_hi[:, k, :], start=k == 0, stop=False)
                        mm(out, w_hi[:, slot, cols], x_lo[:, k, :], start=False, stop=False)
                        last = mm(out, w_lo[:, slot, cols], x_hi[:, k, :], start=False, stop=k == KD - 1)
                last.then_inc(unit_used, 1)

            def unit_tm(m, c, u, bank0, x_hi, x_lo, nk, wait_x=None):
                slot = m % RING
                pe.wait_ge(lo_ready, CU * c + (m + 1))
                for kk in range(2):
                    k = 2 * u + kk
                    if wait_x is not None:
                        wait_x(k)
                    cols = slice(kk * WCOLS, (kk + 1) * WCOLS)
                    for t in range(NTOK):
                        out, tt = ps[:, bank0 + t, :], slice(t * P, (t + 1) * P)
                        mm(out, x_hi[:, k, tt], w_hi[:, slot, cols], start=k == 0, stop=False)
                        mm(out, x_hi[:, k, tt], w_lo[:, slot, cols], start=False, stop=False)
                        last = mm(out, x_lo[:, k, tt], w_hi[:, slot, cols], start=False, stop=k == nk - 1)
                last.then_inc(unit_used, 1)

            def transpose_x(n, src, ready):
                for t in range(NTOK):
                    pe.wait_ge(*at(ready, t + 1 if n else 32))
                    for k in range(KD):
                        ins = nc.tensor.transpose(ps[:, k, t * P:(t + 1) * P], src[:, t, k * P:(k + 1) * P], ident[:, :])
                        if t == NTOK - 1:
                            ins.then_inc(TR[n]["done"][0], 1)

            def x_ready(n):
                return lambda k: pe.wait_ge(*at(TR[n]["lo"], max(k + 1, 4)))

            def ffn(i):
                f, s = FFN[i], START[i]

                def chunk(c, k):
                    if not (iv(c) and c < 2):
                        pe.wait_ge(*at(f["h32"], c - 1))
                    for u in range(CU):
                        unit_fm(s["up"] + u, c, u, 4 * k, xT_hi, xT_lo, x_ready(2 * i + 1) if iv(c) and c == 0 else None)

                chunk(0, 0)
                chunk(1, 1)
                with pe.Fori(2, CF - 1, 2) as c:
                    chunk(c, 0)
                    chunk(c + 1, 1)
                chunk(CF - 1, 0)
                pe.wait_ge(*at(f["h32"], CF - 1))
                for h in range(2):
                    if h:
                        pe.wait_ge(*at(f["h32"], CF))
                    for u in range(CF):
                        if h == 0:
                            pe.wait_ge(*at(f["lo"], u + 1))
                        unit_tm(s["down"] + h * CF + u, 0, u, 4 * (1 - h), hT_hi, hT_lo, KF)

            def out_product(i, wait_x=None):
                for h in range(2):
                    for u in range(CU):
                        unit_tm(START[i]["out"] + h * CU + u, 0, u, 4 * h, xT_hi, xT_lo, KD, wait_x if h == 0 else None)

            def fox(i, j):
                f, m0 = FOX[i], START[i]["mix"]
                for c in range(2):
                    for u in range(CU):
                        unit_fm(m0 + CU * c + u, 0, u, 4 * c, xT_hi, xT_lo, x_ready(2 * i) if c == 0 else None)
                with pe.Fori(0, 2) as w:
                    for h in range(2):
                        pe.wait_ge(*at(f["ev_dve" if h else "ev_act"], w + 1))
                        for u in range(CU):
                            unit_tm(m0 + (2 + h) * CU + u, 2 * w, u, 4 * h, xT_hi, xT_lo, KD)
                pe.wait_ge(*at(f["wf_lo"], 1))
                pe.wait_ge(*at(f["ev_dve"], 1))
                for t in range(NTOK):
                    out, tt = ps[:, 7, t * HEADS:(t + 1) * HEADS], slice(t * P, (t + 1) * P)
                    for k in range(KD):
                        mm(out, xT_hi[:, k, tt], wf_hi[:, k, :], start=k == 0, stop=False)
                        mm(out, xT_hi[:, k, tt], wf_lo[:, k, :], start=False, stop=False)
                        last = mm(out, xT_lo[:, k, tt], wf_hi[:, k, :], start=False, stop=k == KD - 1)
                last.then_inc(f["fproj"][0], 1)
                pe.wait_ge(*at(f["ev_act"], 3))
                pe.wait_ge(*at(f["ev_dve"], 3))
                pe.wait_ge(*at(f["z"], 1))
                for k in range(KD):
                    for t in range(NTOK):
                        ins = nc.tensor.transpose(ps[:, k, t * P:(t + 1) * P], kv_tok[:, 0, t, k * P:(k + 1) * P], ident[:, :])
                    ins.then_inc(f["kT_done"][0], 1)
                pe.wait_ge(*at(f["lf"], 1))
                pe.wait_ge(*at(f["lfc_in"], 16))
                pe.wait_ge(*at(f["kT_a"], 4))
                pe.wait_ge(*at(f["kT_d"], 4))
                for t in range(NTOK):
                    nc.tensor.transpose(ps[0:HEADS, 0, t * P:(t + 1) * P], lf_tok[:, t, :], ident[:, :])
                for n in range(2 * DB):
                    ins = nc.tensor.transpose(ps[0:HEADS, 4 + n // 4, (n % 4) * P:(n % 4 + 1) * P], lfc[:, n, :], ident[:, :])
                ins.then_inc(f["lfT_done"][0], 1)
                pe.wait_ge(*at(f["c"], 1))

                def p_scores(it, s):
                    pe.wait_ge(*at(f["staged"], 4 * it + (s + 1)))
                    for lo, hi, off, q in ((0, P, 0, 0), (0, SEQ, P, 1)):
                        out = ps[:, s, off:off + hi]
                        mm(out, sel[:, s, :], cp[:, 0:hi], start=True, stop=False, skip_group_check=True)
                        mm(out.unsqueeze(1), q_s[:, s, q * P:(q + 1) * P], kT[:, ds(2 * it + s // 2, 1), 0:hi],
                           start=False, stop=False, skip_group_check=True)
                        last = mm(ps[:, s, off + hi - P:off + hi], ident[:, :], causal[:, :], start=False, stop=True,
                                  skip_group_check=True)
                    last.then_inc(f["scores"][0], 1)

                def p_turn(it, s):
                    pe.wait_ge(*at(f["exp"], 4 * it + (s + 1)))
                    for n in range(3):
                        ins = nc.tensor.transpose(ps[:, 4 + s % 2, n * P:(n + 1) * P], p_p[:, s, n * P:(n + 1) * P],
                                                  ident[:, :])
                    ins.then_inc(f["pT"][0], 1)

                def p_out(it, s):
                    pe.wait_ge(*at(f["pT_ev"], 4 * it + (s + 1)))
                    if s >= 2:
                        pe.wait_ge(*at(f["o_ev"], 4 * it + (s - 1)))
                    pT, bank, cols = pT_p[:, s % 2, :], 6 + s % 2, ds(4 * HD * it + HD * s, HD)
                    mm(ps[:, bank, 0:HD], pT[:, 0:P], kv_tok[:, 1, 0, cols], start=True, stop=True)
                    mm(ps[:, bank, HD:2 * HD], pT[:, P:2 * P], kv_tok[:, 1, 0, cols], start=True, stop=False)
                    mm(ps[:, bank, HD:2 * HD], pT[:, 2 * P:T], kv_tok[:, 1, 1, cols], start=False, stop=True).then_inc(
                        f["o"][0], 1)

                with pe.Fori(0, 4) as it:
                    p_scores(it, 0)
                    p_scores(it, 1)
                    p_turn(it, 0)
                    p_scores(it, 2)
                    p_out(it, 0)
                    p_turn(it, 1)
                    p_scores(it, 3)
                    p_out(it, 1)
                    p_turn(it, 2)
                    p_out(it, 2)
                    p_turn(it, 3)
                    p_out(it, 3)
                    pe.wait_ge(*at(f["o_ev"], 4 * it + 4))
                for k in range(KD):
                    for t in range(2):
                        ins = nc.tensor.transpose(ps[:, k, t * P:(t + 1) * P], o_tok[:, t, k * P:(k + 1) * P], ident[:, :])
                    ins.then_inc(f["oT"][0], 1)
                pe.wait_ge(*at(f["c"], 1 + DB))
                pe.wait_ge(*at(f["heads8"], 1))
                pe.wait_ge(*at(f["oT_lo"], KD))

                def s_keys(it, t):
                    b2, hf = t // 2, t % 2
                    if hf == 0:
                        pe.wait_ge(*at(f[f"kv{b2}"], 32 * it + 32))
                    for g in range(4):
                        for n in range(2):
                            ins = nc.tensor.transpose(
                                ps[:, g // 2, (g % 2) * PAST + n * P:(g % 2) * PAST + (n + 1) * P],
                                k_c[b2][:, n, (4 * hf + g) * P:(4 * hf + g + 1) * P], ident[:, :])
                    ins.then_inc(f["ktr"][0], 1)

                def s_scores(it, t):
                    b2, hf, bank = t // 2, t % 2, 2 + t % 2
                    if hf == 0:
                        pe.wait_ge(*at(f["qst"], 2 * it + (b2 + 1)))
                    pe.wait_ge(*at(f["kt_a"], 4 * it + (t + 1)))
                    pe.wait_ge(*at(f["kt_d"], 4 * it + (t + 1)))
                    for g in range(4):
                        rows, k = slice(32 * g, 32 * g + 32), 4 * hf + g
                        q = qbd[:, b2, k, :, :].rearrange("p e q -> p (e q)")
                        mm(ps[rows, bank, 0:PAST], q, ktc[:, k, :], start=True, stop=False, skip_group_check=True)
                        mm(ps[rows, bank, PAST:PAST + DT], q, k_new[:, b2, k, :], start=False, stop=False,
                           skip_group_check=True)
                    mm(ps[:, bank, PAST:PAST + DT], ident[:, :], new_mask[:, :], start=False, stop=False,
                       skip_group_check=True)
                    mm(ps[:, bank, 0:PAST + DT].unsqueeze(1), heads8[:, hf, :], craw[:, ds(2 * it + b2, 1), :],
                       start=False, stop=True, skip_group_check=True).then_inc(f["s_scores"][0], 1)

                def s_turn(it, t):
                    hf = t % 2
                    pe.wait_ge(*at(f["s_p"], 4 * it + (t + 1)))
                    for n in range(3):
                        ins = nc.tensor.transpose(ps[:, 4 + hf, n * P:(n + 1) * P], p_s[:, hf, n * P:(n + 1) * P], ident[:, :])
                    ins.then_inc(f["s_pT"][0], 1)

                def s_out(it, t):
                    b2, hf = t // 2, t % 2
                    pe.wait_ge(*at(f["s_pT_ev"], 4 * it + (t + 1)))
                    if t >= 2:
                        pe.wait_ge(*at(f["s_o_lo"], 4 * it + (t - 1)))
                    for g in range(4):
                        k = 4 * hf + g
                        out, cols = ps[:, 6 + hf, 32 * g:32 * g + 32], slice(k * P, (k + 1) * P)
                        for n in range(3):
                            v = kv_tok[:, 1, 2, cols] if n == 2 else v_c[b2][:, n, cols]
                            last = mm(out, v, pT_s[:, hf, n * P + 32 * g:n * P + 32 * g + 32], start=n == 0, stop=n == 2)
                    last.then_inc(f["s_o"][0], 1)

                with pe.Fori(0, 4) as it:
                    for t in range(4):
                        s_keys(it, t)
                        s_scores(it, t)
                        if t >= 1:
                            s_turn(it, t - 1)
                            s_out(it, t - 1)
                    s_turn(it, 3)
                    s_out(it, 3)
                    pe.wait_ge(*at(f["s_o_lo"], 4 * it + 4))
                out_product(i)

            def hgrn(i, j):
                f, m0 = HGR[i], START[i]["mix"]
                for c in range(4):
                    if c >= 2:
                        pe.wait_ge(*at(f["ev"], c - 1))
                    for u in range(CU):
                        unit_fm(m0 + CU * c + u, 0, u, 4 * (c % 2), xT_hi, xT_lo, x_ready(2 * i) if c == 0 else None)
                with pe.Fori(0, 2) as w:
                    for h in range(2):
                        pe.wait_ge(*at(f["ev"], 2 * w + (h + 3)))
                        for u in range(CU):
                            unit_tm(m0 + (4 + h) * CU + u, 2 * w, u, 4 * h, xT_hi, xT_lo, KD)
                pe.wait_ge(*at(f["ev"], 8))

                def head(h2, s):
                    h = 2 * h2 + s
                    col = ds(P * h, P)
                    pe.wait_ge(*at(f["k2"], h + 1))
                    for t in range(NTOK):
                        ins = nc.tensor.transpose(ps[:, 4, t * P:(t + 1) * P], k2[:, t * P:(t + 1) * P], ident[:, :])
                    ins.then_inc(f["k2T"][0], 1)
                    pe.wait_ge(*at(f["lq"], h + 1))

                    def pairs(t):
                        tt, bank = slice(t * P, (t + 1) * P), 2 * (t % 2)
                        mm(ps[:, bank, 0:P].unsqueeze(1), k_h[:, tt], qT[:, ds(h, 1), tt], start=True, stop=True)
                        for n in range(TILE_LEVELS[t]):
                            side = lev[:, LOFF[n] + t * P:LOFF[n] + (t + 1) * P]
                            last = mm(ps[:, bank + (n + 1) // 4, ((n + 1) % 4) * P:((n + 1) % 4 + 1) * P], side, side,
                                      start=True, stop=True)
                        last.then_inc(f["sc"][0], 1)

                    def outputs(t):
                        pe.wait_ge(*at(f["scm"], NTOK * h + (t + 1)))
                        n = TILE_LEVELS[t] + 1
                        for l in range(n):
                            mm(ps[:, 5, t * P:(t + 1) * P], sc[:, t % 2, l, :], vg[:, 0, t, col], start=l == 0,
                               stop=t == 0 and l == n - 1)

                    pairs(0)
                    pairs(1)
                    pe.wait_ge(*at(f["k2T_ev"], h + 1))
                    mm(ps[:, 4, T:T + P], k2T[:, 0:P], vg[:, 0, 0, col], start=True, stop=True).then_inc(f["s1"][0], 1)
                    if not (iv(h2) and h2 == 0 and s == 0):
                        pe.wait_ge(*at(f["out"], h))
                        pe.wait_ge(*at(f["snew"], h))
                    outputs(0)
                    pairs(2)
                    outputs(1)
                    pe.wait_ge(*at(f["s1_ev"], h + 1))
                    mm(ps[:, 5, P:2 * P], q_e[:, P:2 * P], s1[:, :], start=False, stop=True)
                    outputs(2)
                    pe.wait_ge(*at(f[f"st{s}_in"], 16 * h2 + 16))
                    pe.wait_ge(*at(f["qb"], h + 1))
                    for b in range(DB):
                        mm(ps[:, 5, 2 * P:T], q_blk[:, b, :], S_b[:, s, b, :], start=False, stop=b == DB - 1)
                    mm(ps[:, 5, T:T + P], k2T[:, P:2 * P], vg[:, 0, 1, col], start=True, stop=True).then_inc(f["sfin"][0], 1)
                    pe.wait_ge(*at(f["vm"], h + 1))
                    for a in range(2):
                        ins = mm(ps[:, 6 + a, :], k2T[:, 2 * P:T], v_m[:, 4 * a:4 * a + 4, :], start=True, stop=True)
                    ins.then_inc(f["upd"][0], 1)
                    nc.tensor.transpose(ps[:, 4, 0:P], ident[:, :], ident[:, :]).then_inc(f["o"][0], 1)

                head(0, 0)
                head(0, 1)
                with pe.Fori(1, 4) as h2:
                    head(h2, 0)
                    head(h2, 1)
                pe.wait_ge(*at(f["out"], HG))
                pe.wait_ge(*at(f["snew"], HG))
                for k in range(KD):
                    for t in range(NTOK):
                        ins = nc.tensor.transpose(ps[:, k, t * P:(t + 1) * P], vg[:, 0, t, k * P:(k + 1) * P], ident[:, :])
                    ins.then_inc(f["oT"][0], 1)
                pe.wait_ge(*at(f["oT_lo"], KD))
                out_product(i)

            def pool(i, j):
                f, m0 = POOL[i], START[i]["out"]
                pe.wait_ge(*at(f["in"], 32))
                pe.wait_ge(*at(f["ext"], 2 * KD))
                for k in range(KD):
                    nc.tensor.transpose(ps[:, k, 0:DB * HIST], hist[:, k * P:(k + 1) * P],
                                        ident[0:DB * HIST, 0:DB * HIST]).then_inc(f["hist_T"][0], 1)
                pe.wait_ge(*at(f["hist_ev"], KD))
                for h in range(2):
                    m = m0 + h
                    pe.wait_ge(lo_ready, m + 1)
                    for gg in range(2):
                        g = 2 * h + gg
                        pe.wait_ge(*at(f["lo"], g + 1))
                        for t in range(NTOK):
                            out, tt = ps[:, 4 * h + t, gg * 256:(gg + 1) * 256], slice(t * P, (t + 1) * P)
                            for kk in range(2):
                                cols = slice(kk * WCOLS + gg * 256, kk * WCOLS + (gg + 1) * 256)
                                k = 2 * g + kk
                                mm(out, xT_hi[:, k, tt], w_hi[:, m % RING, cols], start=kk == 0, stop=False)
                                mm(out, xT_hi[:, k, tt], w_lo[:, m % RING, cols], start=False, stop=False)
                                last = mm(out, xT_lo[:, k, tt], w_hi[:, m % RING, cols], start=False, stop=kk == 1)
                    last.then_inc(unit_used, 1)

            pe.wait_ge(ident_ready, 2)
            pe.wait_ge(mask_loaded, 16 * KD)
            pe.wait_ge(rows_loaded, 48)
            for k in range(KD):
                nc.tensor.transpose(ps[:, 6, k * 4 * DEPTH:(k + 1) * 4 * DEPTH], gb_rows[:, k * P:(k + 1) * P],
                                    ident[0:4 * DEPTH, 0:4 * DEPTH])
                ins = nc.tensor.transpose(ps[:, 7, k * DEPTH:(k + 1) * DEPTH], lb_rows[:, k * P:(k + 1) * P],
                                          ident[0:DEPTH, 0:DEPTH])
            ins.then_inc(rowsT_done, 1)
            pe.wait_ge(gbT_ready, 2)
            transpose_x(0, x_tok, (x_loaded, 0))
            for i in range(DEPTH):
                kind = KINDS[i % 3]
                {"fox": fox, "hgrn": hgrn, "pool": pool}[kind](i, i // 3)
                pe.wait_ge(*at(LN[2 * i]["resid"], 2 * NTOK))
                transpose_x(2 * i + 1, xn, LN[2 * i]["xn"])
                ffn(i)
                if i + 1 < DEPTH:
                    pe.wait_ge(*at(LN[2 * i + 1]["resid"], 2 * NTOK))
                    transpose_x(2 * i + 2, xn, LN[2 * i + 1]["xn"])


_INS = ["x_prompt", "x_sample", "cache_fox_k", "cache_fox_v", "cache_fox_lf", "state_hgrn", "cache_pool",
        "w_fox_in", "b_fox_f", "w_fox_out", "w_hgrn_in", "hgrn_lb", "hgrn_norm_g", "w_hgrn_out",
        "w_pool", "pool_scale", "w_ffn_in", "w_ffn_out", "ln_g", "ln_b"]
_OUTS = [(1, 256, 1024), (8, 16, 1024), (2, 1, 256, 16, 64), (2, 1, 256, 16, 64), (2, 1, 256, 16), (1, 1, 8, 128, 128),
         (1, 1, 15, 1024), (2, 8, 16, 16, 64), (2, 8, 16, 16, 64), (2, 8, 16, 16), (1, 8, 8, 128, 128), (1, 8, 15, 1024)]


def kernel(**inputs):
    import numpy as _np
    import concourse.bacc as _bacc
    from concourse import mybir as _mybir
    from concourse.bass_utils import run_bass_kernel_spmd as _run

    nc = _bacc.Bacc("TRN2", target_bir_lowering=False, num_devices=1)
    arrays, args = {}, []
    for name in _INS:
        a = _np.ascontiguousarray(inputs[name])
        arrays[f"in_{name}_dram"] = a
        args.append(nc.dram_tensor(f"in_{name}_dram", a.shape, _mybir.dt.from_np(a.dtype), kind="ExternalInput").ap())
    for i, shape in enumerate(_OUTS):
        args.append(nc.dram_tensor(f"out_{i}_dram", shape, _mybir.dt.float32, kind="ExternalOutput").ap())
    trunk_program(nc, *args)
    r = _run(nc, [arrays], core_ids=[0])
    return tuple(r.results[0][f"out_{i}_dram"] for i in range(len(_OUTS)))
```

```python
from contextlib import ExitStack

import concourse.bass as bass
from concourse import mybir

F32 = mybir.dt.float32
F32R = mybir.dt.float32r
I32 = mybir.dt.int32
ALU = mybir.AluOpType
ACT = mybir.ActivationFunctionType
AX_X = mybir.AxisListType.X

D = 1024
P = 128
KD = D // P
SEQ, DB, DT, PAST = 256, 8, 16, 256
NTOK = 3
T = NTOK * P
DEPTH = 4
KINDS = ("fox", "hgrn", "pool")
HEADS, HD = 16, 64
HG = 8
HIST = 15
FF = ((8 * D + 3 * 256 - 1) // (3 * 256)) * 256
KF = FF // P
ALPHA = (2 * DEPTH) ** 0.25
SCALE = HD ** -0.5
LN_EPS, RMS_EPS = 1e-5, 1e-6
MASKED = -1e30
NEWTON = 3
RSQRT = 3 + 3 * NEWTON

RING = 4
WCOLS = 512
CU = D // (2 * P)
CF = KF // 2

LEVELS = (1, 2, 4, 8, 16, 32, 64)
LCOLS = [T if 2 * m <= DT else SEQ for m in LEVELS]
LOFF = [sum(LCOLS[:n]) for n in range(len(LEVELS))]
LALL = sum(LCOLS)
TILE_LEVELS = (7, 7, 4)


def phase_starts():
    starts, n = [], 0
    for i in range(DEPTH):
        kind = KINDS[i % 3]
        s = {"mix": n}
        n += {"fox": 6 * CU, "hgrn": 8 * CU, "pool": 0}[kind]
        s["out"] = n
        n += 2 if kind == "pool" else 2 * CU
        s["up"] = n
        n += CF * CU
        s["down"] = n
        n += 2 * CF
        starts.append(s)
    return starts, n


def trunk_program(nc, x_prompt, x_sample, cache_fox_k, cache_fox_v, cache_fox_lf, state_hgrn, cache_pool,
                  w_fox_in, b_fox_f, w_fox_out, w_hgrn_in, hgrn_lb, hgrn_norm_g, w_hgrn_out,
                  w_pool, pool_scale, w_ffn_in, w_ffn_out, ln_g, ln_b,
                  y_prompt, y_sample, fox_k_prompt, fox_v_prompt, fox_lf_prompt, hgrn_state_prompt, pool_prompt,
                  fox_k_sample, fox_v_sample, fox_lf_sample, hgrn_state_sample, pool_sample):
    ds = bass.ds
    START, UNITS = phase_starts()
    LN_LAST = 2 * DEPTH - 1

    with ExitStack() as ctx:
        place = {}

        def sb(name, shape, offset, dt=F32):
            size = 4
            for s in shape[1:]:
                size *= s
            size = -(-size // 32) * 32
            place[name] = offset + size
            return nc.alloc_sbuf_tensor_at(name, shape, dt, offset=offset)

        def after(name):
            return place[name]

        def sem(name):
            return ctx.enter_context(nc.semaphore(name))

        base = -(-nc.sbuf_base // 64) * 64
        w_raw = sb("w_raw", [P, RING, 2 * WCOLS], base)
        w_hi = sb("w_hi", [P, RING, 2 * WCOLS], after("w_raw"), F32R)
        w_lo = sb("w_lo", [P, RING, 2 * WCOLS], after("w_hi"), F32R)
        x_tok = sb("x_tok", [P, NTOK, D], after("w_lo"))
        gb = sb("gb", [P, 2, D], after("x_tok"))
        ident = sb("ident", [P, P], after("gb"))
        causal = sb("causal", [P, P], after("ident"))
        new_mask = sb("new_mask", [P, DT], after("causal"))
        half = sb("half", [P, 2], after("new_mask"))
        own = sb("own", [P, 2, HD], after("half"))
        gbT = sb("gbT", [P, KD, 4 * DEPTH], after("own"))
        lbT = sb("lbT", [P, KD, DEPTH], after("gbT"))
        lb_col = sb("lb_col", [P, KD], after("lbT"))
        oml_col = sb("oml_col", [P, KD], after("lb_col"))
        lb_max = sb("lb_max", [P, KD], after("oml_col"))
        lb_sum = sb("lb_sum", [P, KD], after("lb_max"))
        stats = sb("stats", [P, NTOK, 2, 6], after("lb_sum"))
        mv = sb("mv", [P, NTOK, 2], after("stats"))
        rstd = sb("rstd", [P, NTOK], after("mv"))
        var = sb("var", [P, NTOK], after("rstd"))
        nt = sb("nt", [P, NTOK], after("var"))
        t32 = sb("t32", [P, 2, T], after("nt"))
        xT_hi = sb("xT_hi", [P, KD, T], after("t32"), F32R)
        xT_lo = sb("xT_lo", [P, KD, T], after("xT_hi"), F32R)
        xn = sb("xn", [P, NTOK, D], after("xT_lo"))
        qT = sb("qT", [P, KD, T], after("xT_lo"))
        u0 = after("xn")
        hT_hi = sb("hT_hi", [P, KF, T], u0, F32R)
        hT_lo = sb("hT_lo", [P, KF, T], after("hT_hi"), F32R)
        sg = sb("sg", [P, 2, 2, T], after("hT_lo"))
        h32 = sb("h32", [P, 2, 2, T], after("sg"))
        kT = sb("kT", [P, KD, T], u0)
        kv_tok = sb("kv_tok", [P, 2, NTOK, D], after("kT"))
        o_tok = kv_tok[:, 0, 0:2, :]
        craw = sb("craw", [HEADS, DB, PAST + DT], after("kv_tok"))
        cp = sb("cp", [HEADS, SEQ], after("craw"))
        wf_hi = sb("wf_hi", [P, KD, HEADS], after("cp"), F32R)
        wf_lo = sb("wf_lo", [P, KD, HEADS], after("wf_hi"), F32R)
        heads8 = sb("heads8", [HEADS, 2, P], after("cp"))
        bf = sb("bf", [P, HEADS], after("wf_lo"))
        z = sb("z", [P, NTOK, HEADS], after("bf"))
        za = sb("za", [P, NTOK, HEADS], after("z"))
        zm = sb("zm", [P, NTOK, HEADS], after("za"))
        lf_tok = sb("lf_tok", [P, NTOK, HEADS], after("zm"))
        qbd = sb("qbd", [P, 2, KD, 2, DT], after("lf_tok"))
        k_new = sb("k_new", [P, 2, KD, DT], after("qbd"))
        p_s = sb("p_s", [P, 2, T], after("k_new"))
        pT_s = sb("pT_s", [P, 2, T], after("p_s"))
        x_s = sb("x_s", [P, 2, P], after("pT_s"))
        o_s = sb("o_s", [P, 4, DT], after("x_s"))
        mx = sb("mx", [P, 4, 2], after("o_s"))
        nmx = sb("nmx", [P, 4, 2], after("mx"))
        rs = sb("rs", [P, 4, 2], after("nmx"))
        rt = sb("rt", [P, 4], after("rs"))
        rcp = sb("rcp", [P, 4, 2], after("rt"))
        k_c0 = sb("k_c0", [P, 2, D], after("rcp"))
        v_c0 = sb("v_c0", [P, 2, D], after("k_c0"))
        k_c1 = sb("k_c1", [P, 2, D], after("v_c0"))
        v_c1 = sb("v_c1", [P, 2, D], after("k_c1"))
        ktc = sb("ktc", [P, KD, PAST], after("v_c1"))
        ones = sb("ones", [HEADS, PAST + DT], after("v_c1"))
        wf = sb("wf", [P, KD, HEADS], after("ones"))
        lfc = sb("lfc", [P, DB * 2, HEADS], after("wf"))
        k_c, v_c = (k_c0, k_c1), (v_c0, v_c1)
        q_s = sb("q_s", [P, 4, SEQ], after("v_c0"))
        sel = sb("sel", [HEADS, 4, P], after("q_s"))
        p_p = sb("p_p", [P, 4, T], after("sel"))
        pT_p = sb("pT_p", [P, 2, T], after("p_p"))
        sp = sb("sp", [P, HG, T], u0)
        sn = sb("sn", [P, HG, T], after("sp"))
        vg = sb("vg", [P, 2, NTOK, D], after("sn"))
        S_b = sb("S_b", [P, 2, DB, P], after("vg"))
        b_h = sb("b_h", [P, T], after("S_b"))
        k_h = sb("k_h", [P, 2, T], after("b_h"))
        e_b = sb("e_b", [P, 2, T], after("k_h"))
        e_l = sb("e_l", [P, T], after("e_b"))
        q_e = sb("q_e", [P, 2, T], after("e_l"))
        k2 = sb("k2", [P, T], after("q_e"))
        k2T = sb("k2T", [P, T], after("k2"))
        q_blk = sb("q_blk", [P, 2, DB, P], after("k2T"))
        s1 = sb("s1", [P, P], after("q_blk"))
        s_fin = sb("s_fin", [P, 2, P], after("s1"))
        ng = sb("ng", [P, P], after("s_fin"))
        row_m = sb("row_m", [P, DB], after("ng"))
        cut = sb("cut", [P, T], after("row_m"))
        lmask = sb("lmask", [P, 8, P], after("cut"))
        ss = sb("ss", [P, NTOK], after("lmask"))
        rr = sb("rr", [P, NTOK], after("ss"))
        sq = sb("sq", [P, P], after("rr"))
        lev = sb("lev", [P, 2, LALL], after("t32"))
        sc = sb("sc", [P, 2, 8, P], after("sq"))
        sc2 = sb("sc2", [P, TILE_LEVELS[2] + 1, P], after("sc"))
        v_m = sb("v_m", [P, DB, P], after("lev"))
        assert after("v_m") <= after("xT_lo")
        ext_p = sb("ext_p", [P, KD, HIST + SEQ], u0)
        ext_s = sb("ext_s", [P, KD, DB, HIST + DT], after("ext_p"))
        wp = [sb(f"wp{n}", [P, 2, HIST + SEQ], after("ext_s") if n == 0 else after(f"wp{n-1}")) for n in range(2)]
        ws = [sb(f"ws{n}", [P, 2, DB, HIST + DT], after("wp1") if n == 0 else after(f"ws{n-1}")) for n in range(2)]
        zp = sb("zp", [P, KD, T], after("ws1"))
        cnt = sb("cnt", [P, DT], after("zp"))
        scale_bc = sb("scale_bc", [P, D], after("cnt"))
        hist = sb("hist", [DB * HIST, D], after("scale_bc"))
        zq = sb("zq", [P, 2, DT], after("hist"))
        ysc = sb("ysc", [P, 2, WCOLS], after("zq"))
        for name, end in place.items():
            assert end <= nc.sbuf_usable_end, (name, end, nc.sbuf_usable_end)
        gb_rows = sb("gb_rows", [4 * DEPTH, D], u0)
        lb_rows = sb("lb_rows", [DEPTH, D], after("gb_rows"))

        ps = ctx.enter_context(nc.psum_tensor("ps", [P, 8, 512], F32))

        raw_loaded = [sem(f"raw_loaded{n}") for n in range(RING)]
        hi_ready = sem("hi_ready")
        lo_ready = sem("lo_ready")
        unit_used = sem("unit_used")
        x_loaded = sem("x_loaded")
        rows_loaded = sem("rows_loaded")
        const_set = sem("const_set")
        mask_loaded = sem("mask_loaded")
        ident_ready = sem("ident_ready")
        rowsT_done = sem("rowsT_done")
        gbT_ready = sem("gbT_ready")
        lb_steps = sem("lb_steps")
        gb_loaded = sem("gb_loaded")
        def marks(prefix, turns, counts, skipped=()):
            sems = {k: sem(f"{prefix}_{k}") for k in counts}
            return [{k: (sems[k], sum(c for m in range(n) if (k, m) not in skipped)) for k, c in counts.items()}
                    for n in range(turns)]

        def at(mark, value):
            return mark[0], value + mark[1]

        pooled = [2 * i for i in range(DEPTH) if KINDS[i % 3] == "pool"]
        LN = marks("ln", 2 * DEPTH, {"tile": NTOK - 1, "resid": 2 * NTOK, "stat": NTOK, "aggr": NTOK, "rstd": RSQRT, "xn": NTOK,
                                     "gx": NTOK, "x": NTOK}, [("tile", n) for n in pooled])
        TR = marks("tr", 2 * DEPTH, {"done": KD, "t32": KD, "hi": KD, "lo": KD},
                   [(k, n) for k in ("t32", "hi", "lo") for n in pooled])
        FFN = marks("ffn", DEPTH, {k: CF for k in ("silu", "h32", "hi", "lo")})
        fox_layers = [i for i in range(DEPTH) if KINDS[i % 3] == "fox"]
        FOX = dict(zip(fox_layers, marks("fox", len(fox_layers), {
            "wf_in": 16, "bf_in": 16, "lfc_in": 16, "wf_hi": 1, "wf_lo": 1, "ev_act": 3, "ev_dve": 3, "fproj": 1, "z": 1,
            "zma": 2, "ze": 1, "zl": 1, "lf": 1, "kT_done": KD, "kT_a": KD // 2, "kT_d": KD // 2, "lfT_done": 1,
            "ones": 1, "heads8": 1, "c_raw": 3, "c": 1 + DB, 
            **{k: HEADS for k in ("staged", "scores", "max", "nmax", "exp", "rcp", "pT", "pT_ev", "o", "o_ev")},
            "oT": KD, "oT_32": KD, "oT_hi": KD, "oT_lo": KD, **{k: 16 * (DB // 2) for k in ("k0", "k1", "v0", "v1")}, "qst": DB,
            **{k: 2 * DB for k in ("ktr", "kt_a", "kt_d", "s_scores", "s_max", "s_nmax", "s_exp", "s_sum", "s_rcp",
                                   "s_pT", "s_pT_ev", "s_o", "s_x", "s_xT", "s_half", "s_os", "s_hi", "s_lo")},
            "stored": 16 * 6})))
        HGR = {i: {k: (sem(f"hgrn_{k}"), 0) for k in (
            "consts", "pconst", "masks", "ng_in", "ev", "gate", "g", "k", "b", "sub", "expl", "expb", "lq", "qe",
            "k2", "k2T", "k2T_ev", "qb", "vm", "sc", "scm", "s1", "s1_ev", "sfin", "sfin_ev", "o", "ss", "rr", "out",
            "st0_in", "st1_in", "upd", "snew", "stored0", "stored1", "pstored0", "pstored1", "oT", "oT_32", "oT_hi", "oT_lo")}
            for i in range(DEPTH) if KINDS[i % 3] == "hgrn"}
        POOL = {i: {k: (sem(f"pool_{k}"), 0) for k in (
            "in", "consts", "hist_ev", "ext", "w", "z", "hi", "lo", "ysc", "stored")}
            for i in range(DEPTH) if KINDS[i % 3] == "pool"}
        y_stored = sem("y_stored")

        block = ctx.enter_context(nc.Block())

        def iv(x):
            return isinstance(x, int)

        def pipeline(eng, total, step, ahead=0, behind=0):
            def run(i, s):
                step(i, s, (lambda d: 0 <= 4 * i + s + d < total) if iv(i) else (lambda d: True))

            for s in range(4):
                run(0, s)
            last = total // 4 - (1 if ahead else 0)
            with eng.Fori(1, last) as i:
                for s in range(4):
                    run(i, s)
            for i in range(last, total // 4):
                for s in range(4):
                    run(i, s)
            for s in range(behind):
                run(total // 4, s)

        def head_pairs(eng, head):
            for s in range(2):
                head(s, s)
            with eng.Fori(1, HG // 2 - 1) as h2:
                for s in range(2):
                    head(2 * h2 + s, s)
            for s in range(2):
                head(HG - 2 + s, s)

        @block.sync
        def _(sync):
            def load(m, c, parts):
                if not iv(c) or m + CU * c >= RING:
                    sync.wait_ge(lo_ready, CU * c + (m - RING + 1))
                for kk in range(2):
                    dst, src = parts(kk)
                    sync.dma_start(dst, src).then_inc(raw_loaded[m % RING], 16)

            def square(w, m, c, u, cols):
                slot = m % RING
                rows = w.rearrange("(u kk p) n -> u kk p n", kk=2, p=P)
                load(m, c, lambda kk: (w_raw[:, slot, kk * WCOLS:(kk + 1) * WCOLS], rows[u, kk, :, ds(cols, WCOLS)]))

            def chunks(w, m0, n):
                first = 0
                if m0 == 0:
                    for u in range(CU):
                        square(w, u, 0, u, 0)
                    first = 1
                with sync.Fori(first, n) as c:
                    for u in range(CU):
                        square(w, m0 + u, c, u, c * WCOLS)

            sync.dma_start(x_tok[:, 0:2, :], x_prompt.rearrange("b (a p) d -> p (b a) d", p=P)).then_inc(x_loaded, 16)
            sync.dma_start(x_tok[:, 2, :], x_sample.rearrange("b t d -> (b t) d")).then_inc(x_loaded, 16)
            for i in range(DEPTH):
                kind, j, s = KINDS[i % 3], i // 3, START[i]
                if kind == "fox":
                    chunks(w_fox_in[j], s["mix"], 6)
                    chunks(w_fox_out[j], s["out"], 2)
                elif kind == "hgrn":
                    chunks(w_hgrn_in[j], s["mix"], 8)
                    chunks(w_hgrn_out[j], s["out"], 2)
                else:
                    for u in range(2):
                        m = s["out"] + u
                        load(m, 0, lambda kk: (
                            w_raw[:, m % RING, kk * WCOLS:(kk + 1) * WCOLS].rearrange("p (g c) -> p g c", g=2),
                            w_pool[j, 2 * u:2 * u + 2, kk * P:(kk + 1) * P, :].rearrange("g p c -> p g c")))
                up = w_ffn_in[i].rearrange("(u kk p) (a n) -> u kk p a n", kk=2, p=P, a=2)
                with sync.Fori(0, CF) as c:
                    for u in range(CU):
                        slot = (s["up"] + u) % RING
                        load(s["up"] + u, c, lambda kk: (
                            w_raw[:, slot, kk * WCOLS:(kk + 1) * WCOLS].rearrange("p (a n) -> p a n", a=2),
                            up[u, kk, :, :, ds(c * 256, 256)]))
                for h in range(2):
                    for u in range(CF):
                        square(w_ffn_out[i], s["down"] + h * CF + u, 0, u, h * WCOLS)

        @block.scalar
        def _(act):
            def w_hi_of(m, c=0):
                if iv(c) and m + CU * c >= UNITS:
                    return
                slot = m % RING
                act.wait_ge(raw_loaded[slot], 32 * c + 32 * (m // RING + 1))
                if not iv(c) or m + CU * c >= RING:
                    act.wait_ge(unit_used, CU * c + (m - RING + 1))
                nc.scalar.activation(w_hi[:, slot, :], w_raw[:, slot, :], ACT.Copy).then_inc(hi_ready, 1)

            def ahead(m0, c=0):
                for u in range(CU):
                    w_hi_of(m0 + RING + u, c)

            def transposed(done, t32_at, lo, n=0, width=T, affine=False):
                for k in range(KD):
                    act.wait_ge(*at(done, k + 1))
                    if k >= 2:
                        act.wait_ge(*at(lo, k - 1))
                    nc.scalar.activation(t32[:, k % 2, 0:width], ps[:, k, 0:width], ACT.Identity,
                                         bias=gbT[:, k, n + 2 * DEPTH - 1:n + 2 * DEPTH] if affine else 0.0,
                                         scale=gbT[:, k, n - 1:n] if affine else 1.0).then_inc(t32_at[0], 1)

            def ffn(i):
                f, m0 = FFN[i], START[i]["up"]

                def chunk(c, k):
                    ahead(m0, c)
                    act.wait_ge(unit_used, CU * c + (m0 + CU))
                    if not (iv(c) and c < 2):
                        act.wait_ge(*at(f["h32"], c - 1))
                    nc.scalar.activation(sg[:, k], ps[:, 4 * k:4 * k + 2, 0:T], ACT.Silu).then_inc(f["silu"][0], 1)
                    act.wait_ge(*at(f["h32"], c + 1))
                    nc.scalar.activation(hT_hi[:, ds(2 * c, 2), :], h32[:, k], ACT.Copy).then_inc(f["hi"][0], 1)

                chunk(0, 0)
                chunk(1, 1)
                with act.Fori(2, CF - 1, 2) as c:
                    chunk(c, 0)
                    chunk(c + 1, 1)
                chunk(CF - 1, 0)
                for u in range(2 * CF):
                    w_hi_of(START[i]["down"] + u + RING)

            def fox(i, j):
                f, m0 = FOX[i], START[i]["mix"]
                ahead(m0)
                act.wait_ge(unit_used, m0 + CU)
                if i:
                    act.wait_ge(*at(LN[2 * i - 1]["x"], NTOK))
                nc.scalar.activation(qT[:, 0:4, :], ps[:, 0:4, 0:T], ACT.Copy).then_inc(f["ev_act"][0], 1)
                act.wait_ge(*at(f["wf_in"], 16))
                nc.scalar.activation(wf_hi[:, :, :], wf[:, :, :], ACT.Copy).then_inc(f["wf_hi"][0], 1)
                ahead(m0 + CU)
                with act.Fori(0, 2) as w:
                    for h in range(2):
                        for u in range(CU):
                            w_hi_of(m0 + (2 + h) * CU + RING + u, 2 * w)
                        if h == 0:
                            act.wait_ge(unit_used, 2 * CU * w + (m0 + 3 * CU))
                            nc.scalar.activation(kv_tok[:, ds(w, 1), :, 0:WCOLS],
                                                 ps[:, 0:3, :], ACT.Copy).then_inc(f["ev_act"][0], 1)
                for k in range(0, KD, 2):
                    act.wait_ge(*at(f["kT_done"], k + 1))
                    nc.scalar.activation(kT[:, k, :], ps[:, k, 0:T], ACT.Copy).then_inc(f["kT_a"][0], 1)
                act.wait_ge(*at(f["zma"], 2))
                nc.scalar.activation(za[:, :, :], za[:, :, :], ACT.Exp, scale=-1.0).then_inc(f["ze"][0], 1)
                act.wait_ge(*at(f["ze"], 1))
                nc.scalar.activation(z[:, :, :], za[:, :, :], ACT.Ln, bias=1.0).then_inc(f["zl"][0], 1)
                def prompt(it, s, live):
                    if live(0):
                        act.wait_ge(*at(f["nmax"], 4 * it + (s + 1)))
                        for q, lo, hi in ((0, 0, P), (1, P, T)):
                            ins = nc.scalar.activation(p_p[:, s, lo:hi], ps[:, s, lo:hi], ACT.Exp, bias=nmx[:, s, q:q + 1],
                                                       scale=SCALE, accum_out=rs[:, s, q:q + 1])
                        ins.then_inc(f["exp"][0], 1)
                    if live(-1):
                        act.wait_ge(*at(f["pT"], 4 * it + s))
                        nc.scalar.activation(pT_p[:, (s - 1) % 2, :], ps[:, 4 + (s - 1) % 2, 0:T],
                                             ACT.Copy).then_inc(f["pT_ev"][0], 1)

                pipeline(act, HEADS, prompt, behind=1)
                transposed(f["oT"], f["oT_32"], f["oT_lo"], width=SEQ)

                def keys(it, s):
                    hf = s % 2
                    act.wait_ge(*at(f["ktr"], 4 * it + (s + 1)))
                    nc.scalar.activation(ktc[:, 4 * hf:4 * hf + 2, :],
                                         ps[:, 2 * hf, :].rearrange("p (g s) -> p g s", g=2),
                                         ACT.Copy).then_inc(f["kt_a"][0], 1)

                def sample(it, s, live):
                    if iv(it) and 4 * it + s == 0:
                        keys(0, 0)
                    if live(1):
                        keys(it, s + 1)
                    if live(-1):
                        act.wait_ge(*at(f["s_pT"], 4 * it + s))
                        nc.scalar.activation(pT_s[:, (s - 1) % 2, :], ps[:, 6, 0:T], ACT.Copy).then_inc(f["s_pT_ev"][0], 1)
                    if live(0):
                        hf, bank = s % 2, 4 + s % 2
                        act.wait_ge(*at(f["s_nmax"], 4 * it + (s + 1)))
                        nc.scalar.activation(p_s[:, hf, 0:PAST], ps[:, bank, 0:PAST], ACT.Exp, bias=nmx[:, hf, 0:1],
                                             scale=SCALE, accum_out=rs[:, hf, 0:1])
                        nc.scalar.activation(p_s[:, hf, ds(2 * DT * it + (DT * (s // 2) + PAST), DT)],
                                             ps[:, bank, PAST:PAST + DT], ACT.Exp, bias=nmx[:, hf, 0:1],
                                             scale=SCALE, accum_out=rs[:, hf, 1:2]).then_inc(f["s_exp"][0], 1)

                pipeline(act, 2 * DB, sample, ahead=1, behind=1)
                ahead(START[i]["out"])
                ahead(START[i]["out"] + CU)

            def hgrn(i, j):
                f, m0 = HGR[i], START[i]["mix"]
                for c in range(8):
                    ahead(m0 + CU * c)
                    act.wait_ge(unit_used, m0 + CU * (c + 1))
                    b0 = 4 * (c % 2)
                    h4 = slice(4 * (c % 2), 4 * (c % 2) + 4)
                    cols = slice(WCOLS * (c % 2), WCOLS * (c % 2) + WCOLS)
                    if c < 2:
                        if c == 0:
                            act.wait_ge(*at(LN[2 * i - 1]["x"], NTOK))
                        nc.scalar.activation(qT[:, h4, :], ps[:, b0:b0 + 4, 0:T], ACT.Silu).then_inc(f["ev"][0], 1)
                    elif c < 4:
                        nc.scalar.activation(sp[:, h4, :], ps[:, b0:b0 + 4, 0:T], ACT.Sigmoid)
                        nc.scalar.activation(sn[:, h4, :], ps[:, b0:b0 + 4, 0:T], ACT.Sigmoid,
                                             scale=-1.0).then_inc(f["ev"][0], 1)
                    elif c < 6:
                        nc.scalar.activation(vg[:, 0, :, cols], ps[:, b0:b0 + 3, :], ACT.Copy).then_inc(f["ev"][0], 1)
                    else:
                        nc.scalar.activation(vg[:, 1, :, cols], ps[:, b0:b0 + 3, :], ACT.Silu).then_inc(f["ev"][0], 1)
                act.wait_ge(*at(f["ev"], 8))

                def gates(h, s):
                    nc.scalar.activation(b_h[:, :], sp[:, ds(h, 1), :], ACT.Ln, bias=lb_col[:, ds(h, 1)],
                                         scale=oml_col[:, ds(h, 1)]).then_inc(f["g"][0], 1)
                    act.wait_ge(*at(f["b"], h + 1))
                    nc.scalar.activation(e_b[:, s, :], b_h[:, :], ACT.Exp).then_inc(f["expb"][0], 1)
                    act.wait_ge(*at(f["sub"], 8 * h + 8))
                    nc.scalar.activation(e_l[:, :], e_l[:, :], ACT.Exp).then_inc(f["expb"][0], 1)
                    nc.scalar.activation(lev[:, s, :], lev[:, s, :], ACT.Exp).then_inc(f["expl"][0], 1)

                def squares(h):
                    act.wait_ge(*at(f["o"], h + 1))
                    for t in range(NTOK):
                        nc.scalar.activation(sq[:, :], ps[:, 5, t * P:(t + 1) * P], ACT.Square,
                                             accum_out=ss[:, t:t + 1]).then_inc(f["ss"][0], 1)
                        act.wait_ge(*at(f["ss"], NTOK * h + (t + 1)))

                def head(h, s):
                    if not (iv(h) and h == 0):
                        squares(h + (-1))
                    act.wait_ge(*at(f["k2T"], h + 1))
                    nc.scalar.activation(k2T[:, :], ps[:, 4, 0:T], ACT.Copy).then_inc(f["k2T_ev"][0], 1)
                    if not (iv(h) and h == HG - 1):
                        gates(h + 1, 1 - s)

                gates(0, 0)
                head_pairs(act, head)
                squares(HG - 1)
                transposed(f["oT"], f["oT_32"], f["oT_lo"])
                ahead(START[i]["out"])
                ahead(START[i]["out"] + CU)

            def pool(i, j):
                f = POOL[i]
                for k in range(KD):
                    act.wait_ge(*at(TR[2 * i]["done"], k + 1))
                    nc.scalar.activation(ext_s[:, k, :, 0:HIST],
                                         ps[:, k, T:T + DB * HIST].rearrange("p (b r) -> p b r", b=DB),
                                         ACT.Copy).then_inc(f["hist_ev"][0], 1)
                    for dst, src in ((ext_p[:, k, HIST:], ps[:, k, 0:SEQ]),
                                     (ext_s[:, k, :, HIST:], ps[:, k, SEQ:T].rearrange("p (b t) -> p b t", b=DB))):
                        nc.scalar.activation(dst, src, ACT.Identity,
                                             bias=gbT[:, k, 2 * i + 2 * DEPTH - 1:2 * i + 2 * DEPTH],
                                             scale=gbT[:, k, 2 * i - 1:2 * i]).then_inc(f["ext"][0], 1)
                for g in range(4):
                    act.wait_ge(*at(f["z"], g + 1))
                    nc.scalar.activation(xT_hi[:, 2 * g:2 * g + 2, :], zp[:, 2 * g:2 * g + 2, :],
                                         ACT.Copy).then_inc(f["hi"][0], 1)
                for u in range(2):
                    w_hi_of(START[i]["out"] + RING + u)

            for u in range(RING):
                w_hi_of(u)
            act.wait_ge(lb_steps, 2)
            nc.scalar.activation(lbT[:, :, :], lbT[:, :, :], ACT.Exp).then_inc(lb_steps, 1)
            def transposed_x(n):
                transposed(TR[n]["done"], TR[n]["t32"], TR[n]["lo"], n, affine=n > 0)

            transposed_x(0)
            for i in range(DEPTH):
                {"fox": fox, "hgrn": hgrn, "pool": pool}[KINDS[i % 3]](i, i // 3)
                transposed_x(2 * i + 1)
                if i % 3 == 0:
                    act.wait_ge(*at(FOX[i]["stored"], 16 * 6))
                elif i % 3 == 1:
                    for k in ("stored0", "stored1", "pstored0", "pstored1"):
                        act.wait_ge(*at(HGR[i][k], 16 * (HG // 2)))
                ffn(i)
                if i + 1 < DEPTH and KINDS[(i + 1) % 3] != "pool":
                    transposed_x(2 * i + 2)

        @block.vector
        def _(dve):
            V = nc.vector

            def w_lo_of(m, c=0):
                if iv(c) and m + CU * c >= UNITS:
                    return
                slot = m % RING
                dve.wait_ge(hi_ready, CU * c + (m + 1))
                V.tensor_tensor(w_lo[:, slot, :], w_raw[:, slot, :], w_hi[:, slot, :].bitcast(F32),
                                ALU.subtract).then_inc(lo_ready, 1)

            def ahead(m0, c=0):
                for u in range(CU):
                    w_lo_of(m0 + RING + u, c)

            def split(t32_at, hi, lo, width=T):
                for k in range(KD):
                    dve.wait_ge(*at(t32_at, k + 1))
                    V.tensor_copy(xT_hi[:, k, 0:width], t32[:, k % 2, 0:width]).then_inc(hi[0], 1)
                    dve.wait_ge(*at(hi, k + 1))
                    V.tensor_tensor(xT_lo[:, k, 0:width], t32[:, k % 2, 0:width], xT_hi[:, k, 0:width].bitcast(F32),
                                    ALU.subtract).then_inc(lo[0], 1)

            def split_x(n):
                split(TR[n]["t32"], TR[n]["hi"], TR[n]["lo"])

            def rsqrt(v, r, mark, before):
                dve.wait_ge(*at(mark, before + 1))
                V.tensor_scalar(r.bitcast(I32), v.bitcast(I32), 1, None, ALU.logical_shift_right).then_inc(mark[0], 1)
                dve.wait_ge(*at(mark, before + 2))
                V.tensor_scalar(r.bitcast(I32), r.bitcast(I32), -1.0, float(0x5F3759DF), ALU.mult,
                                ALU.add).then_inc(mark[0], 1)
                for n in range(NEWTON):
                    dve.wait_ge(*at(mark, before + 3 + 3 * n))
                    V.scalar_tensor_tensor(out=nt[:, :], in0=r, scalar=-0.5, in1=r, op0=ALU.mult,
                                           op1=ALU.mult).then_inc(mark[0], 1)
                    dve.wait_ge(*at(mark, before + 4 + 3 * n))
                    V.tensor_tensor(nt[:, :], nt[:, :], v, ALU.mult).then_inc(mark[0], 1)
                    dve.wait_ge(*at(mark, before + 5 + 3 * n))
                    V.scalar_tensor_tensor(out=r, in0=nt[:, :], scalar=1.5, in1=r, op0=ALU.add,
                                           op1=ALU.mult).then_inc(mark[0], 1)

            def residual_half(n, h, bank0, ready, scaled=None):
                ln, cols = LN[n], slice(h * WCOLS, (h + 1) * WCOLS)
                if n and h == 0:
                    dve.wait_ge(*at(LN[n - 1]["x"], NTOK))
                for t in range(NTOK):
                    y, k = ps[:, bank0 + t, :], NTOK * h + t
                    ready(t)
                    if scaled is not None:
                        if k >= 2:
                            dve.wait_ge(*at(ln["resid"], k - 1))
                        V.tensor_tensor(ysc[:, k % 2, :], y, scale_bc[:, cols], ALU.mult).then_inc(scaled[0], 1)
                        dve.wait_ge(*at(scaled, k + 1))
                        y = ysc[:, k % 2, :]
                    V.scalar_tensor_tensor(out=xn[:, t, cols], in0=x_tok[:, t, cols], scalar=ALPHA, in1=y,
                                           op0=ALU.mult, op1=ALU.add).then_inc(ln["resid"][0], 1)
                    dve.wait_ge(*at(ln["resid"], k + 1))
                    ins = V.bn_stats(stats[:, t, h, :], xn[:, t, cols])
                    if h == 1:
                        ins.then_inc(ln["stat"][0], 1)

            def normalise(n):
                ln = LN[n]
                for t in range(NTOK):
                    dve.wait_ge(*at(ln["stat"], t + 1))
                    V.bn_aggr(mv[:, t, :], stats[:, t, :, :].rearrange("p a b -> p (a b)")).then_inc(ln["aggr"][0], 1)
                dve.wait_ge(*at(ln["aggr"], NTOK))
                V.tensor_scalar(var[:, :], mv[:, :, 1], LN_EPS, None, ALU.add).then_inc(ln["rstd"][0], 1)
                rsqrt(var[:, :], rstd[:, :], ln["rstd"], 0)
                for t in range(NTOK):
                    dve.wait_ge(*at(ln["rstd"], RSQRT))
                    V.tensor_scalar(xn[:, t, :], xn[:, t, :], mv[:, t, 0:1], rstd[:, t:t + 1], ALU.subtract,
                                    ALU.mult).then_inc(ln["xn"][0], 1)

            def product_and_norm(n, start, units, bank0):
                split_at = units + 1
                for u in range(split_at):
                    w_lo_of(start + u + RING)
                residual_half(n, 0, bank0[0], lambda t: dve.wait_ge(unit_used, start + units))
                for u in range(split_at, 2 * units - 2):
                    w_lo_of(start + u + RING)
                residual_half(n, 1, bank0[1], lambda t: dve.wait_ge(*at(LN[n]["tile"], t + 1)) if t < NTOK - 1
                              else dve.wait_ge(unit_used, start + 2 * units))
                normalise(n)
                for u in range(2 * units - 2, 2 * units):
                    w_lo_of(start + u + RING)

            def ffn(i):
                f, m0 = FFN[i], START[i]["up"]

                def chunk(c, k):
                    ahead(m0, c)
                    dve.wait_ge(*at(f["silu"], c + 1))
                    if not (iv(c) and c < 2):
                        dve.wait_ge(*at(f["hi"], c - 1))
                        dve.wait_ge(*at(f["lo"], c - 1))
                    V.tensor_tensor(h32[:, k], sg[:, k], ps[:, 4 * k + 2:4 * k + 4, 0:T],
                                    ALU.mult).then_inc(f["h32"][0], 1)
                    dve.wait_ge(*at(f["hi"], c + 1))
                    V.tensor_tensor(hT_lo[:, ds(2 * c, 2), :], h32[:, k], hT_hi[:, ds(2 * c, 2), :].bitcast(F32),
                                    ALU.subtract).then_inc(f["lo"][0], 1)

                chunk(0, 0)
                chunk(1, 1)
                with dve.Fori(2, CF - 1, 2) as c:
                    chunk(c, 0)
                    chunk(c + 1, 1)
                chunk(CF - 1, 0)

            def fox(i, j):
                f, m0 = FOX[i], START[i]["mix"]
                V.memset(ones[:, :], 1.0).then_inc(f["ones"][0], 1)
                ahead(m0)
                ahead(m0 + CU)
                dve.wait_ge(unit_used, m0 + 2 * CU)
                V.tensor_copy(qT[:, 4:8, :], ps[:, 4:8, 0:T]).then_inc(f["ev_dve"][0], 1)
                dve.wait_ge(*at(f["wf_hi"], 1))
                V.tensor_tensor(wf_lo[:, :, :], wf[:, :, :], wf_hi[:, :, :].bitcast(F32),
                                ALU.subtract).then_inc(f["wf_lo"][0], 1)
                with dve.Fori(0, 2) as w:
                    for h in range(2):
                        for u in range(CU):
                            w_lo_of(m0 + (2 + h) * CU + RING + u, 2 * w)
                    dve.wait_ge(unit_used, 2 * CU * w + (m0 + 4 * CU))
                    V.tensor_copy(kv_tok[:, ds(w, 1), :, WCOLS:D], ps[:, 4:7, :]).then_inc(f["ev_dve"][0], 1)
                dve.wait_ge(*at(f["fproj"], 1))
                dve.wait_ge(*at(f["bf_in"], 16))
                V.tensor_tensor(z[:, :, :], ps[:, 7, 0:NTOK * HEADS].rearrange("p (t h) -> p t h", t=NTOK),
                                bf[:, :].unsqueeze(1).broadcast_to([P, NTOK, HEADS]), ALU.add).then_inc(f["z"][0], 1)
                dve.wait_ge(*at(f["z"], 1))
                V.tensor_scalar(zm[:, :, :], z[:, :, :], 0.0, None, ALU.min).then_inc(f["zma"][0], 1)
                V.scalar_tensor_tensor(out=za[:, :, :], in0=z[:, :, :], scalar=-1.0, in1=z[:, :, :], op0=ALU.mult,
                                       op1=ALU.max).then_inc(f["zma"][0], 1)
                dve.wait_ge(*at(f["zl"], 1))
                V.tensor_tensor(lf_tok[:, :, :], zm[:, :, :], z[:, :, :], ALU.subtract).then_inc(f["lf"][0], 1)
                for k in range(1, KD, 2):
                    dve.wait_ge(*at(f["kT_done"], k + 1))
                    V.tensor_copy(kT[:, k, :], ps[:, k, 0:T]).then_inc(f["kT_d"][0], 1)
                for hf in range(2):
                    ins = V.tensor_copy(heads8[:, hf, :].rearrange("p (h q) -> p h q", q=DT),
                                        ident[0:HEADS, 8 * hf:8 * hf + 8].unsqueeze(2).broadcast_to([HEADS, 8, DT]))
                ins.then_inc(f["heads8"][0], 1)
                dve.wait_ge(*at(f["lfT_done"], 1))
                V.tensor_scalar(cp[:, :], ps[0:HEADS, 0, 0:SEQ], -1.0 / SCALE, None, ALU.mult).then_inc(f["c_raw"][0], 1)
                V.tensor_scalar(craw[:, :, PAST:], ps[0:HEADS, 0, SEQ:T].rearrange("p (b t) -> p b t", b=DB),
                                -1.0 / SCALE, None, ALU.mult).then_inc(f["c_raw"][0], 1)
                V.tensor_scalar(craw[:, :, 0:PAST], ps[0:HEADS, 4:8, :].rearrange("p a (b t) -> p (a b) t", b=2),
                                -1.0 / SCALE, None, ALU.mult).then_inc(f["c_raw"][0], 1)
                dve.wait_ge(*at(f["c_raw"], 3))
                dve.wait_ge(*at(f["ones"], 1))
                V.tensor_tensor_scan(cp[:, :], ones[:, 0:SEQ], cp[:, :], 0.0, ALU.mult, ALU.add).then_inc(f["c"][0], 1)
                for b in range(DB):
                    V.tensor_tensor_scan(craw[:, b, :], ones[:, :], craw[:, b, :], 0.0, ALU.mult,
                                         ALU.add).then_inc(f["c"][0], 1)

                dve.wait_ge(*at(f["stored"], 16 * 6))

                def prompt_max(it, s):
                    dve.wait_ge(*at(f["scores"], 4 * it + (s + 1)))
                    V.tensor_reduce(mx[:, s, 0:1], ps[:, s, 0:P], AX_X, ALU.max)
                    V.tensor_reduce(mx[:, s, 1:2], ps[:, s, P:T], AX_X, ALU.max).then_inc(f["max"][0], 1)
                    dve.wait_ge(*at(f["max"], 4 * it + (s + 1)))
                    V.tensor_scalar(nmx[:, s, :], mx[:, s, :], -SCALE, None, ALU.mult).then_inc(f["nmax"][0], 1)

                def prompt_out(it, s):
                    z = s % 4
                    dve.wait_ge(*at(f["exp"], 4 * it + (s + 1)))
                    V.reciprocal(rcp[:, z, :], rs[:, z, :]).then_inc(f["rcp"][0], 1)
                    dve.wait_ge(*at(f["rcp"], 4 * it + (s + 1)))
                    dve.wait_ge(*at(f["o"], 4 * it + (s + 1)))
                    for q in range(2):
                        ins = V.tensor_scalar(o_tok[:, q, ds(4 * HD * it + HD * s, HD)],
                                              ps[:, 6 + s % 2, q * HD:(q + 1) * HD],
                                              rcp[:, z, q:q + 1], None, ALU.mult)
                    ins.then_inc(f["o_ev"][0], 1)

                def prompt(it, s, live):
                    if live(0):
                        prompt_max(it, s)
                    if live(-2):
                        prompt_out(it, s - 2)

                pipeline(dve, HEADS, prompt, behind=2)
                split(f["oT_32"], f["oT_hi"], f["oT_lo"], SEQ)

                def keys(it, s):
                    hf = s % 2
                    dve.wait_ge(*at(f["ktr"], 4 * it + (s + 1)))
                    V.tensor_copy(ktc[:, 4 * hf + 2:4 * hf + 4, :],
                                  ps[:, 2 * hf + 1, :].rearrange("p (g s) -> p g s", g=2)).then_inc(f["kt_d"][0], 1)

                def sample_max(it, s):
                    hf = s % 2
                    dve.wait_ge(*at(f["s_scores"], 4 * it + (s + 1)))
                    V.memset(p_s[:, hf, PAST:T], 0.0)
                    V.tensor_reduce(mx[:, hf, 0:1], ps[:, 4 + hf, 0:PAST + DT], AX_X,
                                    ALU.max).then_inc(f["s_max"][0], 1)
                    dve.wait_ge(*at(f["s_max"], 4 * it + (s + 1)))
                    V.tensor_scalar(nmx[:, hf, 0:1], mx[:, hf, 0:1], -SCALE, None, ALU.mult).then_inc(f["s_nmax"][0], 1)

                def own_head(it, s):
                    hf = s % 2
                    dve.wait_ge(*at(f["s_exp"], 4 * it + (s + 1)))
                    V.tensor_tensor(rt[:, hf:hf + 1], rs[:, hf, 0:1], rs[:, hf, 1:2], ALU.add).then_inc(f["s_sum"][0], 1)
                    dve.wait_ge(*at(f["s_sum"], 4 * it + (s + 1)))
                    V.reciprocal(rcp[:, hf, 0:1], rt[:, hf:hf + 1]).then_inc(f["s_rcp"][0], 1)
                    dve.wait_ge(*at(f["s_rcp"], 4 * it + (s + 1)))
                    dve.wait_ge(*at(f["s_o"], 4 * it + (s + 1)))
                    V.scalar_tensor_tensor(out=x_s[:, hf, :], in0=ps[:, 7, 0:P], scalar=rcp[:, hf, 0:1],
                                           in1=own[:, :, :].rearrange("p e d -> p (e d)"), op0=ALU.mult,
                                           op1=ALU.mult).then_inc(f["s_x"][0], 1)

                def fold(it, s):
                    hf = s % 2
                    dst = (slice(4 * hf, 4 * hf + 4), ds(2 * DT * it + (DT * (s // 2) + SEQ), DT))
                    pair = ps[:, 7, P:2 * P].rearrange("p (g e q) -> p g e q", g=4, e=2)
                    dve.wait_ge(*at(f["s_xT"], 4 * it + (s + 1)))
                    V.tensor_copy(o_s[:, :, :], pair[:, :, 0, :]).then_inc(f["s_half"][0], 1)
                    dve.wait_ge(*at(f["s_half"], 4 * it + (s + 1)))
                    V.tensor_tensor(o_s[:, :, :], o_s[:, :, :], pair[:, :, 1, :], ALU.add).then_inc(f["s_os"][0], 1)
                    dve.wait_ge(*at(f["s_os"], 4 * it + (s + 1)))
                    V.tensor_copy(xT_hi[:, dst[0], dst[1]], o_s[:, :, :]).then_inc(f["s_hi"][0], 1)
                    dve.wait_ge(*at(f["s_hi"], 4 * it + (s + 1)))
                    V.tensor_tensor(xT_lo[:, dst[0], dst[1]], o_s[:, :, :], xT_hi[:, dst[0], dst[1]].bitcast(F32),
                                    ALU.subtract).then_inc(f["s_lo"][0], 1)

                def sample(it, s, live):
                    if live(-2):
                        fold(it, s - 2)
                    if iv(it) and 4 * it + s == 0:
                        keys(0, 0)
                    if live(1):
                        keys(it, s + 1)
                    if live(0):
                        sample_max(it, s)
                    if live(-1):
                        own_head(it, s - 1)

                pipeline(dve, 2 * DB, sample, ahead=1, behind=2)

            def hgrn(i, j):
                f, m0 = HGR[i], START[i]["mix"]
                V.memset(cut[:, :], 1.0).then_inc(f["consts"][0], 1)
                V.memset(q_blk[:, :, :, :], 0.0)
                dve.wait_ge(*at(f["consts"], 1))
                V.memset(cut[:, 0:SEQ:P], 0.0)
                V.memset(cut[:, SEQ:T:DT], 0.0).then_inc(f["consts"][0], 1)
                for c in range(8):
                    ahead(m0 + CU * c)
                dve.wait_ge(*at(f["ev"], 8))
                dve.wait_ge(*at(f["consts"], 2))
                dve.wait_ge(*at(f["pconst"], 3))

                def distances(h, s):
                    V.tensor_scalar(k_h[:, s:s + 1, :], sn[:, ds(h, 1), :], oml_col[:, ds(h, 1)], None,
                                    ALU.mult).then_inc(f["k"][0], 1)
                    dve.wait_ge(*at(f["g"], h + 1))
                    V.tensor_tensor_scan(b_h[:, :], cut[:, :], b_h[:, :], 0.0, ALU.mult, ALU.add).then_inc(f["b"][0], 1)
                    dve.wait_ge(*at(f["b"], h + 1))
                    for m, off, n in zip(LEVELS, LOFF, LCOLS):
                        blk = b_h[:, 0:n].rearrange("p (a m) -> p a m", m=2 * m)
                        dst = lev[:, s, off:off + n].rearrange("p (a m) -> p a m", m=2 * m)
                        mid = blk[:, :, m - 1:m].broadcast_to([P, n // (2 * m), m])
                        V.tensor_tensor(dst[:, :, 0:m], mid, blk[:, :, 0:m], ALU.subtract)
                        V.tensor_tensor(dst[:, :, m:2 * m], blk[:, :, m:2 * m], mid, ALU.subtract).then_inc(f["sub"][0], 1)
                    for lo, hi, m in ((0, SEQ, P), (SEQ, T, DT)):
                        blk = b_h[:, lo:hi].rearrange("p (a m) -> p a m", m=m)
                        ins = V.tensor_tensor(e_l[:, lo:hi].rearrange("p (a m) -> p a m", m=m),
                                              blk[:, :, m - 1:m].broadcast_to([P, (hi - lo) // m, m]), blk, ALU.subtract)
                    ins.then_inc(f["sub"][0], 1)

                def operands(h, s, reuse):
                    dve.wait_ge(*at(f["expb"], 2 * h + 2))
                    dve.wait_ge(*at(f["k"], h + 1))
                    if reuse:
                        dve.wait_ge(*at(f["k2T"], h))
                    V.tensor_tensor(k2[:, :], k_h[:, s, :], e_l[:, :], ALU.mult).then_inc(f["k2"][0], 1)
                    V.tensor_tensor(q_e[:, s:s + 1, :], qT[:, ds(h, 1), :], e_b[:, s:s + 1, :],
                                    ALU.mult).then_inc(f["qe"][0], 1)
                    dve.wait_ge(*at(f["expl"], h + 1))
                    for m, off, n in zip(LEVELS, LOFF, LCOLS):
                        w = lev[:, s, off:off + n].rearrange("p (a e m) -> p a e m", e=2, m=m)
                        qv = qT[:, ds(h, 1), 0:n].rearrange("p o (a e m) -> p (o a) e m", e=2, m=m)
                        kv = k_h[:, s, 0:n].rearrange("p (a e m) -> p a e m", e=2, m=m)
                        V.tensor_tensor(w[:, :, 0, :], w[:, :, 0, :], kv[:, :, 0, :], ALU.mult)
                        ins = V.tensor_tensor(w[:, :, 1, :], w[:, :, 1, :], qv[:, :, 1, :], ALU.mult)
                    ins.then_inc(f["lq"][0], 1)
                    dve.wait_ge(*at(f["qe"], h + 1))
                    diag = q_blk[:, s, :, :].rearrange("p b t -> p (b t)")
                    step, some = P + DT, DB - 1
                    V.tensor_copy(diag[:, 0:some * step].rearrange("p (b t) -> p b t", t=step)[:, :, 0:DT],
                                  q_e[:, s, SEQ:SEQ + some * DT].rearrange("p (b t) -> p b t", t=DT))
                    V.tensor_copy(diag[:, some * step:], q_e[:, s, SEQ + some * DT:T]).then_inc(f["qb"][0], 1)

                def mask(h, t):
                    n = TILE_LEVELS[t] + 1
                    dve.wait_ge(*at(f["sc"], NTOK * h + (t + 1)))
                    bank = 2 * (t % 2)
                    nn = [(0, 4), (4, n)] if n > 4 else [(0, n)]
                    for a, (lo, hi) in enumerate(nn):
                        ins = V.tensor_tensor(sc2[:, lo:hi, :] if t == 2 else sc[:, t, lo:hi, :],
                                              ps[:, bank + a, 0:(hi - lo) * P].rearrange("p (l s) -> p l s", s=P),
                                              lmask[:, lo:hi, :], ALU.mult)
                    ins.then_inc(f["scm"][0], 1)

                def prompt_state(h, s, turn):
                    dve.wait_ge(*at(f["sfin"], h + 1))
                    V.tensor_copy(s1[:, :], ps[:, 4, T:T + P]).then_inc(f["s1_ev"][0], 1)
                    dve.wait_ge(*at(f["s1_ev"], h + 1))
                    if turn is not None:
                        dve.wait_ge(*at(f[f"pstored{s}"], turn))
                    V.scalar_tensor_tensor(out=s_fin[:, s, :], in0=s1[:, :], scalar=e_b[:, s, SEQ - 1:SEQ],
                                           in1=ps[:, 4, 0:P], op0=ALU.mult, op1=ALU.add).then_inc(f["sfin_ev"][0], 1)

                def results(h):
                    dve.wait_ge(*at(f["ss"], NTOK * h + NTOK))
                    V.tensor_scalar(var[:, :], ss[:, :], 1.0 / P, RMS_EPS, ALU.mult, ALU.add).then_inc(f["rr"][0], 1)
                    rsqrt(var[:, :], rr[:, :], f["rr"], RSQRT * h)
                    dve.wait_ge(*at(f["rr"], RSQRT * h + RSQRT))
                    dve.wait_ge(*at(f["gate"], 1))
                    dve.wait_ge(*at(f["vm"], h + 1))
                    for t in range(NTOK):
                        ins = V.scalar_tensor_tensor(out=vg[:, 0, t, ds(P * h, P)], in0=ps[:, 5, t * P:(t + 1) * P],
                                                     scalar=rr[:, t:t + 1], in1=vg[:, 1, t, ds(P * h, P)],
                                                     op0=ALU.mult, op1=ALU.mult)
                    ins.then_inc(f["out"][0], 1)

                def sample_states(h, s):
                    dve.wait_ge(*at(f["upd"], h + 1))
                    for b in range(DB):
                        ins = V.scalar_tensor_tensor(
                            out=S_b[:, s, b, :], in0=S_b[:, s, b, :],
                            scalar=e_b[:, s, SEQ + DT * b + DT - 1:SEQ + DT * b + DT],
                            in1=ps[:, 6 + b // 4, (b % 4) * P:(b % 4 + 1) * P], op0=ALU.mult, op1=ALU.add)
                    ins.then_inc(f["snew"][0], 1)

                def head(h, s):
                    if not (iv(h) and h == 0):
                        results(h + (-1))
                    mask(h, 0)
                    mask(h, 1)
                    mask(h, 2)
                    prompt_state(h, s, None if iv(h) and h < 2 else 8 * h + (-8 * s))
                    if not (iv(h) and h == 0):
                        sample_states(h + (-1), 1 - s)
                    if not (iv(h) and h == HG - 1):
                        distances(h + 1, 1 - s)
                        operands(h + 1, 1 - s, True)

                distances(0, 0)
                operands(0, 0, False)
                head_pairs(dve, head)
                results(HG - 1)
                sample_states(HG - 1, (HG - 1) % 2)
                split(f["oT_32"], f["oT_hi"], f["oT_lo"])

            def pool(i, j):
                f = POOL[i]
                V.memset(ext_p[:, :, 0:HIST], 0.0).then_inc(f["w"][0], 1)
                dve.wait_ge(*at(f["consts"], 2))
                step = 1

                def chained(ins):
                    nonlocal step
                    ins.then_inc(f["w"][0], 1)
                    step += 1

                def low_part(g):
                    dve.wait_ge(*at(f["hi"], g + 1))
                    V.tensor_tensor(xT_lo[:, 2 * g:2 * g + 2, :], zp[:, 2 * g:2 * g + 2, :],
                                    xT_hi[:, 2 * g:2 * g + 2, :].bitcast(F32), ALU.subtract).then_inc(f["lo"][0], 1)

                chained(V.reciprocal(cnt[:, :], cnt[:, :]))
                for g in range(4):
                    k2s = slice(2 * g, 2 * g + 2)
                    pp, sss = ext_p[:, k2s, :], ext_s[:, k2s, :, :]
                    dve.wait_ge(*at(f["ext"], 4 * g + 4))
                    dve.wait_ge(*at(f["hist_ev"], 2 * g + 2))
                    for e in range(g + 1):
                        d, lo = 1 << e, (1 << (e + 1)) - 1
                        dve.wait_ge(*at(f["w"], step))
                        po, so = wp[e % 2], ws[e % 2]
                        chained(V.tensor_tensor(po[:, :, lo:], pp[:, :, lo:], pp[:, :, lo - d:HIST + SEQ - d], ALU.add))
                        for kk in range(2):
                            chained(V.tensor_tensor(so[:, kk, :, lo:], sss[:, kk, :, lo:],
                                                    sss[:, kk, :, lo - d:HIST + DT - d], ALU.add))
                        pp, sss = po[:, :, :], so[:, :, :, :]
                    dve.wait_ge(*at(f["w"], step))
                    w = 2 << g
                    chained(V.scalar_tensor_tensor(out=zp[:, k2s, 0:SEQ], in0=pp[:, :, HIST:], scalar=1.0 / w,
                                                   in1=ext_p[:, k2s, HIST:], op0=ALU.mult, op1=ALU.subtract))
                    chained(V.tensor_tensor(zq[:, :, 0:w], pp[:, :, HIST:HIST + w],
                                            cnt[:, 0:w].unsqueeze(1).broadcast_to([P, 2, w]), ALU.mult))
                    dve.wait_ge(*at(f["w"], step))
                    chained(V.tensor_tensor(zp[:, k2s, 0:w], zq[:, :, 0:w], ext_p[:, k2s, HIST:HIST + w], ALU.subtract))
                    for kk in range(2):
                        ins = V.scalar_tensor_tensor(
                            out=zp[:, 2 * g + kk, SEQ:T].rearrange("p (b t) -> p b t", b=DB), in0=sss[:, kk, :, HIST:],
                            scalar=1.0 / w, in1=ext_s[:, 2 * g + kk, :, HIST:], op0=ALU.mult, op1=ALU.subtract)
                        chained(ins)
                    dve.wait_ge(*at(f["w"], step))
                    V.tensor_copy(mv[:, 0, :], mv[:, 0, :]).then_inc(f["z"][0], 1)
                    if g:
                        low_part(g - 1)
                low_part(3)
                for u in range(2):
                    w_lo_of(START[i]["out"] + RING + u)

            V.memset(mv[:, :, :], 0.0)
            for u in range(RING):
                w_lo_of(u)
            dve.wait_ge(rowsT_done, 1)
            V.tensor_copy(gbT[:, :, :], ps[:, 6, 0:KD * 4 * DEPTH].rearrange("p (k r) -> p k r", k=KD)).then_inc(gbT_ready, 1)
            V.tensor_copy(lbT[:, :, :], ps[:, 7, 0:KD * DEPTH].rearrange("p (k r) -> p k r", k=KD)).then_inc(gbT_ready, 1)
            dve.wait_ge(gbT_ready, 2)
            V.tensor_reduce(lb_max[:, :], lbT[:, :, :], AX_X, ALU.max).then_inc(lb_steps, 1)
            dve.wait_ge(lb_steps, 1)
            V.tensor_tensor(lbT[:, :, :], lbT[:, :, :], lb_max[:, :].unsqueeze(2).broadcast_to([P, KD, DEPTH]),
                            ALU.subtract).then_inc(lb_steps, 1)
            dve.wait_ge(lb_steps, 3)
            V.tensor_reduce(lb_sum[:, :], lbT[:, :, :], AX_X, ALU.add).then_inc(lb_steps, 1)
            dve.wait_ge(lb_steps, 4)
            V.reciprocal(lb_sum[:, :], lb_sum[:, :]).then_inc(lb_steps, 1)
            dve.wait_ge(lb_steps, 5)
            V.tensor_tensor(lb_col[:, :], lbT[:, :, 1], lb_sum[:, :], ALU.mult).then_inc(lb_steps, 1)
            dve.wait_ge(lb_steps, 6)
            V.tensor_scalar(oml_col[:, :], lb_col[:, :], -1.0, 1.0, ALU.mult, ALU.add).then_inc(lb_steps, 1)
            split_x(0)
            for i in range(DEPTH):
                s = START[i]
                kind = KINDS[i % 3]
                {"fox": fox, "hgrn": hgrn, "pool": pool}[kind](i, i // 3)
                if kind == "pool":
                    dve.wait_ge(*at(POOL[i]["consts"], 2))
                    dve.wait_ge(*at(POOL[i]["in"], 32))
                    for h in range(2):
                        residual_half(2 * i, h, 4 * h, lambda t: dve.wait_ge(unit_used, s["out"] + h + 1), POOL[i]["ysc"])
                    normalise(2 * i)
                else:
                    product_and_norm(2 * i, s["out"], CU, (0, 4))
                split_x(2 * i + 1)
                ffn(i)
                product_and_norm(2 * i + 1, s["down"], CF, (4, 0))
                if i + 1 < DEPTH and KINDS[(i + 1) % 3] != "pool":
                    split_x(2 * i + 2)

        @block.gpsimd
        def _(pool):
            G = nc.gpsimd

            def lone_wait():
                pool.wait_ge(rowsT_done, 1)

            def load_gb(n):
                pool.dma_start(gb[:, 0, :], ln_g[n // 2, n % 2, :].partition_broadcast(P)).then_inc(gb_loaded, 16)
                pool.dma_start(gb[:, 1, :], ln_b[n // 2, n % 2, :].partition_broadcast(P)).then_inc(gb_loaded, 16)

            def residual(n):
                ln = LN[n]
                pool.wait_ge(gb_loaded, 32 * (n + 1))
                for t in range(NTOK):
                    pool.wait_ge(*at(ln["xn"], t + 1))
                    G.tensor_tensor(x_tok[:, t, :], xn[:, t, :], gb[:, 0, :], ALU.mult).then_inc(ln["gx"][0], 1)
                    pool.wait_ge(*at(ln["gx"], t + 1))
                    G.tensor_tensor(x_tok[:, t, :], x_tok[:, t, :], gb[:, 1, :], ALU.add).then_inc(ln["x"][0], 1)
                pool.wait_ge(*at(ln["x"], NTOK))
                if n < LN_LAST:
                    load_gb(n + 1)

            def fox(i, j):
                f, m0 = FOX[i], START[i]["mix"]
                if i:
                    pool.wait_ge(unit_used, m0)
                pool.dma_start(wf[:, :, :], w_fox_in[j][:, 3 * D:].rearrange("(k p) h -> p k h", p=P)).then_inc(f["wf_in"][0], 16)
                pool.dma_start(bf[:, :], b_fox_f[j].partition_broadcast(P)).then_inc(f["bf_in"][0], 16)
                pool.dma_start(lfc[:, :, :], cache_fox_lf[j].rearrange("b (a p) h -> p (b a) h", p=P)).then_inc(f["lfc_in"][0], 16)

                def load_k(b, s):
                    lone_wait()
                    pool.dma_start(k_c[s][:, :, :].unsqueeze(1),
                                   cache_fox_k[j][ds(b, 1)].rearrange("o (a p) h d -> p o a (h d)", p=P)).then_inc(
                                       f[f"k{s}"][0], 16)

                def load_v(b, s):
                    pool.dma_start(v_c[s][:, :, :].unsqueeze(1),
                                   cache_fox_v[j][ds(b, 1)].rearrange("o (a p) h d -> p o a (h d)", p=P)).then_inc(
                                       f[f"v{s}"][0], 16)

                load_k(0, 0)
                load_v(0, 0)
                pool.wait_ge(*at(f["ev_act"], 3))
                pool.wait_ge(*at(f["ev_dve"], 3))
                for n, (kp, ks) in enumerate(((fox_k_prompt, fox_k_sample), (fox_v_prompt, fox_v_sample))):
                    pool.dma_start(kp[j].rearrange("b (a p) h d -> p (b a) (h d)", p=P),
                                   kv_tok[:, n, 0:2, :]).then_inc(f["stored"][0], 16)
                    pool.dma_start(ks[j].rearrange("b t h d -> (b t) (h d)"), kv_tok[:, n, 2, :]).then_inc(f["stored"][0], 16)
                def stage(it, s):
                    G.tensor_copy(sel[:, s, :], ident[0:HEADS, ds(4 * it + s, 1)].broadcast_to([HEADS, P]))
                    G.tensor_tensor(q_s[:, s:s + 1, :], qT[:, ds(2 * it + s // 2, 1), 0:SEQ],
                                    half[:, s % 2:s % 2 + 1].unsqueeze(2).broadcast_to([P, 1, SEQ]),
                                    ALU.mult).then_inc(f["staged"][0], 1)

                for s in range(4):
                    stage(0, s)
                pool.wait_ge(*at(f["lf"], 1))
                pool.dma_start(fox_lf_prompt[j].rearrange("b (a p) h -> p (b a) h", p=P), lf_tok[:, 0:2, :]).then_inc(
                    f["stored"][0], 16)
                pool.dma_start(fox_lf_sample[j].rearrange("b t h -> (b t) h"), lf_tok[:, 2, :]).then_inc(f["stored"][0], 16)
                with pool.Fori(1, 4) as it:
                    for s in range(4):
                        pool.wait_ge(*at(f["scores"], 4 * it + (s - 3)))
                        stage(it, s)

                def stage_q(b, s):
                    cols = ds(DT * b + SEQ, DT)
                    G.tensor_copy(k_new[:, s, :, :], kT[:, :, cols])
                    for e in range(2):
                        ins = G.tensor_tensor(qbd[:, s, :, e, :], qT[:, :, cols],
                                              half[:, e:e + 1].unsqueeze(2).broadcast_to([P, KD, DT]), ALU.mult)
                    ins.then_inc(f["qst"][0], 1)

                stage_q(0, 0)
                stage_q(1, 1)
                pool.wait_ge(*at(f["oT"], KD))
                load_k(1, 1)
                load_v(1, 1)
                with pool.Fori(1, 4) as it:
                    for s in range(2):
                        pool.wait_ge(*at(f["ktr"], 4 * it + (2 * s - 2)))
                        load_k(2 * it + s, s)
                        pool.wait_ge(*at(f["s_scores"], 4 * it + (2 * s - 2)))
                        stage_q(2 * it + s, s)
                        lone_wait()
                        pool.wait_ge(*at(f["s_o"], 4 * it + (2 * s - 2)))
                        load_v(2 * it + s, s)

            def hgrn(i, j):
                f, m0 = HGR[i], START[i]["mix"]
                pool.wait_ge(unit_used, m0)
                pool.dma_start(ng[:, :], hgrn_norm_g[j].partition_broadcast(P)).then_inc(f["ng_in"][0], 16)

                def load_state(h, s):
                    lone_wait()
                    pool.dma_start(S_b[:, s, :, :].unsqueeze(1),
                                   state_hgrn[j][:, ds(h, 1)].rearrange("b o c v -> c o b v")).then_inc(
                                       f[f"st{s}_in"][0], 16)

                load_state(0, 0)
                load_state(1, 1)
                G.memset(lmask[:, :, :], 1.0).then_inc(f["pconst"][0], 1)
                G.memset(row_m[:, :], 1.0).then_inc(f["pconst"][0], 1)
                pool.wait_ge(*at(f["pconst"], 2))
                k = 0

                def select(view, pattern, base, mult):
                    nonlocal k
                    if k:
                        pool.wait_ge(*at(f["masks"], k))
                    G.affine_select(out=view, in_=view, pattern=pattern, compare_op=ALU.is_ge, fill=0.0, base=base,
                                    channel_multiplier=mult).then_inc(f["masks"][0], 1)
                    k += 1

                select(row_m[:, :], [[-DT, DB]], 0, 1)
                select(row_m[:, :], [[DT, DB]], DT - 1, -1)
                select(lmask[:, 0, :], [[1, P]], 0, -1)
                select(lmask[:, 0, :], [[-1, P]], 0, 1)
                for n, m in enumerate(LEVELS):
                    view = lmask[:, n + 1, :].rearrange("p (a r) -> p a r", r=2 * m)
                    na = P // (2 * m)
                    select(view, [[0, na], [1, 2 * m]], -m, 0)
                    select(view, [[-2 * m, na], [0, 2 * m]], 0, 1)
                    select(view, [[2 * m, na], [0, 2 * m]], m - 1, -1)
                pool.wait_ge(*at(f["masks"], k))
                G.memset(sq[:, :], 0.0).then_inc(f["pconst"][0], 1)
                pool.wait_ge(*at(f["ng_in"], 16))
                pool.wait_ge(*at(f["ev"], 8))
                for t in range(NTOK):
                    v = vg[:, 1, t, :].rearrange("p (h v) -> p h v", h=HG)
                    ins = G.tensor_tensor(v, v, ng[:, :].unsqueeze(1).broadcast_to([P, HG, P]), ALU.mult)
                ins.then_inc(f["gate"][0], 1)

                def store_states(h, s):
                    lone_wait()
                    pool.wait_ge(*at(f["snew"], h + 1))
                    pool.dma_start(hgrn_state_sample[j][:, ds(h, 1)].rearrange("b o c v -> c o b v"),
                                   S_b[:, s, :, :].unsqueeze(1)).then_inc(f[f"stored{s}"][0], 16)

                def head(h, s):
                    if not (iv(h) and h == 0):
                        pool.wait_ge(*at(f["upd"], h))
                    pool.wait_ge(*at(f["g"], h + 1))
                    G.tensor_tensor(v_m[:, :, :], vg[:, 0, 2, ds(P * h, P)].unsqueeze(1).broadcast_to([P, DB, P]),
                                    row_m[:, :].unsqueeze(2).broadcast_to([P, DB, P]), ALU.mult).then_inc(f["vm"][0], 1)
                    lone_wait()
                    pool.wait_ge(*at(f["sfin_ev"], h + 1))
                    pool.dma_start(hgrn_state_prompt[j, 0, ds(h, 1)].rearrange("o c v -> c o v"),
                                   s_fin[:, s:s + 1, :]).then_inc(f[f"pstored{s}"][0], 16)
                    if not (iv(h) and h == 0):
                        store_states(h + (-1), 1 - s)
                        if not (iv(h) and h == HG - 1):
                            pool.wait_ge(*at(f[f"stored{1 - s}"], 8 * h + 8 * s))
                            load_state(h + 1, 1 - s)

                head_pairs(pool, head)
                store_states(HG - 1, (HG - 1) % 2)

            def pooling_inputs(i, j):
                f = POOL[i]
                pool.wait_ge(unit_used, START[i]["out"])
                pool.dma_start(hist[:, :], cache_pool[j].rearrange("b r d -> (b r) d")).then_inc(f["in"][0], 16)
                pool.dma_start(scale_bc[:, :], pool_scale[j].partition_broadcast(P)).then_inc(f["in"][0], 16)
                G.iota(cnt[:, :], [[1, DT]], base=1, channel_multiplier=0,
                       allow_small_or_imprecise_dtypes=True).then_inc(f["consts"][0], 2)

            def pooling(i, j):
                f = POOL[i]
                pool.dma_start(pool_prompt[j, 0], x_tok[P - HIST:P, 1, :]).then_inc(f["stored"][0], 16)
                for b in range(DB):
                    pool.dma_start(pool_sample[j, b], x_tok[DT * b + 1:DT * b + DT, 2, :]).then_inc(f["stored"][0], 16)
                pool.wait_ge(*at(f["stored"], 16 * (DB + 1)))

            pool.dma_start(gb_rows[0:2 * DEPTH, :], ln_g.rearrange("i s d -> (i s) d")).then_inc(rows_loaded, 16)
            pool.dma_start(gb_rows[2 * DEPTH:4 * DEPTH, :], ln_b.rearrange("i s d -> (i s) d")).then_inc(rows_loaded, 16)
            pool.dma_start(lb_rows[:, :], hgrn_lb).then_inc(rows_loaded, 16)
            G.memset(ident[:, :], 0.0).then_inc(const_set, 1)
            G.memset(causal[:, :], 0.0).then_inc(const_set, 1)
            G.memset(new_mask[:, :], 0.0).then_inc(const_set, 1)
            G.memset(half[:, :], 1.0).then_inc(const_set, 1)
            pool.wait_ge(const_set, 4)
            G.affine_select(out=ident[:, :], in_=ident[:, :], compare_op=ALU.not_equal, fill=1.0, base=0,
                            pattern=[[-1, P]], channel_multiplier=1).then_inc(ident_ready, 1)
            G.affine_select(out=causal[:, :], in_=causal[:, :], compare_op=ALU.is_ge, fill=MASKED, base=0,
                            pattern=[[-1, P]], channel_multiplier=1).then_inc(ident_ready, 1)
            G.affine_select(out=half[:, 0:1], in_=half[:, 0:1], compare_op=ALU.is_ge, fill=0.0, base=HD - 1,
                            pattern=[[0, 1]], channel_multiplier=-1).then_inc(ident_ready, 1)
            G.affine_select(out=half[:, 1:2], in_=half[:, 1:2], compare_op=ALU.is_ge, fill=0.0, base=-HD,
                            pattern=[[0, 1]], channel_multiplier=1).then_inc(ident_ready, 1)
            G.memset(own[:, :, :], 1.0).then_inc(const_set, 1)
            pool.wait_ge(const_set, 5)
            G.affine_select(out=own[:, 0, :], in_=own[:, 0, :], compare_op=ALU.is_ge, fill=0.0, base=DT - 1,
                            pattern=[[0, HD]], channel_multiplier=-1).then_inc(ident_ready, 1)
            G.affine_select(out=own[:, 1, :], in_=own[:, 1, :], compare_op=ALU.is_ge, fill=0.0, base=-DT,
                            pattern=[[0, HD]], channel_multiplier=1).then_inc(ident_ready, 1)
            pool.wait_ge(ident_ready, 6)
            for g in range(1, 4):
                pool.dma_start(own[2 * DT * g:2 * DT * g + 2 * DT, :, :], own[0:2 * DT, :, :]).then_inc(mask_loaded, 16)
            for h in range(KD):
                pool.dma_start(new_mask[DT * h:DT * h + DT, :], causal[0:DT, 0:DT]).then_inc(mask_loaded, 16)
            load_gb(0)
            pool.wait_ge(rowsT_done, 1)
            for i in range(DEPTH):
                {"fox": fox, "hgrn": hgrn, "pool": pooling}[KINDS[i % 3]](i, i // 3)
                residual(2 * i)
                if i + 1 < DEPTH and KINDS[(i + 1) % 3] == "pool":
                    pooling_inputs(i + 1, (i + 1) // 3)
                residual(2 * i + 1)
            pool.dma_start(y_prompt.rearrange("b (a p) d -> p (b a) d", p=P), x_tok[:, 0:2, :]).then_inc(y_stored, 16)
            pool.dma_start(y_sample.rearrange("b t d -> (b t) d"), x_tok[:, 2, :]).then_inc(y_stored, 16)
            pool.wait_ge(y_stored, 32)
            for i in FOX:
                pool.wait_ge(*at(FOX[i]["stored"], 16 * 6))
            for i in HGR:
                for k in ("stored0", "stored1", "pstored0", "pstored1"):
                    pool.wait_ge(*at(HGR[i][k], 16 * (HG // 2)))
            for i in POOL:
                pool.wait_ge(*at(POOL[i]["stored"], 16 * (DB + 1)))

        @block.tensor
        def _(pe):
            mm = nc.tensor.matmul

            def unit_fm(m, c, u, bank0, x_hi, x_lo, wait_x=None):
                slot = m % RING
                pe.wait_ge(lo_ready, CU * c + (m + 1))
                for kk in range(2):
                    k = 2 * u + kk
                    if wait_x is not None:
                        wait_x(k)
                    for n in range(4):
                        cols = slice(kk * WCOLS + n * P, kk * WCOLS + (n + 1) * P)
                        out = ps[:, bank0 + n, 0:T]
                        mm(out, w_hi[:, slot, cols], x_hi[:, k, :], start=k == 0, stop=False)
                        mm(out, w_hi[:, slot, cols], x_lo[:, k, :], start=False, stop=False)
                        last = mm(out, w_lo[:, slot, cols], x_hi[:, k, :], start=False, stop=k == KD - 1)
                last.then_inc(unit_used, 1)

            def unit_tm(m, c, u, bank0, x_hi, x_lo, nk, wait_x=None):
                slot = m % RING
                pe.wait_ge(lo_ready, CU * c + (m + 1))
                for kk in range(2):
                    k = 2 * u + kk
                    if wait_x is not None:
                        wait_x(k)
                    cols = slice(kk * WCOLS, (kk + 1) * WCOLS)
                    for t in range(NTOK):
                        out, tt = ps[:, bank0 + t, :], slice(t * P, (t + 1) * P)
                        mm(out, x_hi[:, k, tt], w_hi[:, slot, cols], start=k == 0, stop=False)
                        mm(out, x_hi[:, k, tt], w_lo[:, slot, cols], start=False, stop=False)
                        last = mm(out, x_lo[:, k, tt], w_hi[:, slot, cols], start=False, stop=k == nk - 1)
                last.then_inc(unit_used, 1)

            def last_units_tm(n, m, u, bank0, x_hi, x_lo, nk):
                pe.wait_ge(lo_ready, m + 2)
                for t in range(NTOK):
                    out, tt = ps[:, bank0 + t, :], slice(t * P, (t + 1) * P)
                    for v in range(2):
                        slot = (m + v) % RING
                        for kk in range(2):
                            k, cols = 2 * (u + v) + kk, slice(kk * WCOLS, (kk + 1) * WCOLS)
                            mm(out, x_hi[:, k, tt], w_hi[:, slot, cols], start=False, stop=False)
                            mm(out, x_hi[:, k, tt], w_lo[:, slot, cols], start=False, stop=False)
                            last = mm(out, x_lo[:, k, tt], w_hi[:, slot, cols], start=False, stop=k == nk - 1)
                        if t == NTOK - 1:
                            last.then_inc(unit_used, 1)
                        elif v == 1:
                            last.then_inc(LN[n]["tile"][0], 1)

            def transpose_x(n, src, ready):
                for t in range(NTOK):
                    pe.wait_ge(*at(ready, t + 1 if n else 32))
                    for k in range(KD):
                        ins = nc.tensor.transpose(ps[:, k, t * P:(t + 1) * P], src[:, t, k * P:(k + 1) * P], ident[:, :])
                        if t == NTOK - 1:
                            ins.then_inc(TR[n]["done"][0], 1)

            def x_ready(n):
                return lambda k: pe.wait_ge(*at(TR[n]["lo"], max(k + 1, 4)))

            def ffn(i):
                f, s = FFN[i], START[i]

                def chunk(c, k):
                    if not (iv(c) and c < 2):
                        pe.wait_ge(*at(f["h32"], c - 1))
                    for u in range(CU):
                        unit_fm(s["up"] + u, c, u, 4 * k, xT_hi, xT_lo, x_ready(2 * i + 1) if iv(c) and c == 0 else None)

                chunk(0, 0)
                chunk(1, 1)
                with pe.Fori(2, CF - 1, 2) as c:
                    chunk(c, 0)
                    chunk(c + 1, 1)
                chunk(CF - 1, 0)
                pe.wait_ge(*at(f["h32"], CF - 1))
                for h in range(2):
                    if h:
                        pe.wait_ge(*at(f["h32"], CF))
                    for u in range(CF):
                        if h == 0:
                            pe.wait_ge(*at(f["lo"], u + 1))
                        if h == 0 or u < CF - 2:
                            unit_tm(s["down"] + h * CF + u, 0, u, 4 * (1 - h), hT_hi, hT_lo, KF)
                last_units_tm(2 * i + 1, s["down"] + 2 * CF - 2, CF - 2, 0, hT_hi, hT_lo, KF)

            def out_product(i, wait_x=None):
                for h in range(2):
                    for u in range(CU if h == 0 else CU - 2):
                        unit_tm(START[i]["out"] + h * CU + u, 0, u, 4 * h, xT_hi, xT_lo, KD, wait_x if h == 0 else None)
                last_units_tm(2 * i, START[i]["out"] + 2 * CU - 2, CU - 2, 4, xT_hi, xT_lo, KD)

            def fox(i, j):
                f, m0 = FOX[i], START[i]["mix"]
                for c in range(2):
                    for u in range(CU):
                        unit_fm(m0 + CU * c + u, 0, u, 4 * c, xT_hi, xT_lo, x_ready(2 * i) if c == 0 else None)
                with pe.Fori(0, 2) as w:
                    for h in range(2):
                        pe.wait_ge(*at(f["ev_dve" if h else "ev_act"], w + 1))
                        for u in range(CU):
                            unit_tm(m0 + (2 + h) * CU + u, 2 * w, u, 4 * h, xT_hi, xT_lo, KD)
                pe.wait_ge(*at(f["wf_lo"], 1))
                pe.wait_ge(*at(f["ev_dve"], 1))
                for t in range(NTOK):
                    out, tt = ps[:, 7, t * HEADS:(t + 1) * HEADS], slice(t * P, (t + 1) * P)
                    for k in range(KD):
                        mm(out, xT_hi[:, k, tt], wf_hi[:, k, :], start=k == 0, stop=False)
                        mm(out, xT_hi[:, k, tt], wf_lo[:, k, :], start=False, stop=False)
                        last = mm(out, xT_lo[:, k, tt], wf_hi[:, k, :], start=False, stop=k == KD - 1)
                last.then_inc(f["fproj"][0], 1)
                pe.wait_ge(*at(f["ev_act"], 3))
                pe.wait_ge(*at(f["ev_dve"], 3))
                pe.wait_ge(*at(f["z"], 1))
                for k in range(KD):
                    for t in range(NTOK):
                        ins = nc.tensor.transpose(ps[:, k, t * P:(t + 1) * P], kv_tok[:, 0, t, k * P:(k + 1) * P], ident[:, :])
                    ins.then_inc(f["kT_done"][0], 1)
                pe.wait_ge(*at(f["lf"], 1))
                pe.wait_ge(*at(f["lfc_in"], 16))
                pe.wait_ge(*at(f["kT_a"], 4))
                pe.wait_ge(*at(f["kT_d"], 4))
                for t in range(NTOK):
                    nc.tensor.transpose(ps[0:HEADS, 0, t * P:(t + 1) * P], lf_tok[:, t, :], ident[:, :])
                for n in range(2 * DB):
                    ins = nc.tensor.transpose(ps[0:HEADS, 4 + n // 4, (n % 4) * P:(n % 4 + 1) * P], lfc[:, n, :], ident[:, :])
                ins.then_inc(f["lfT_done"][0], 1)
                pe.wait_ge(*at(f["c"], 1))

                def p_scores(it, s):
                    pe.wait_ge(*at(f["staged"], 4 * it + (s + 1)))
                    for lo, hi, off, q in ((0, P, 0, 0), (0, SEQ, P, 1)):
                        out = ps[:, s, off:off + hi]
                        mm(out, sel[:, s, :], cp[:, 0:hi], start=True, stop=False, skip_group_check=True)
                        mm(out.unsqueeze(1), q_s[:, s, q * P:(q + 1) * P], kT[:, ds(2 * it + s // 2, 1), 0:hi],
                           start=False, stop=False, skip_group_check=True)
                        last = mm(ps[:, s, off + hi - P:off + hi], ident[:, :], causal[:, :], start=False, stop=True,
                                  skip_group_check=True)
                    last.then_inc(f["scores"][0], 1)

                def p_turn(it, s):
                    pe.wait_ge(*at(f["exp"], 4 * it + (s + 1)))
                    for n in range(3):
                        ins = nc.tensor.transpose(ps[:, 4 + s % 2, n * P:(n + 1) * P], p_p[:, s % 4, n * P:(n + 1) * P],
                                                  ident[:, :])
                    ins.then_inc(f["pT"][0], 1)

                def p_out(it, s, reuse):
                    pe.wait_ge(*at(f["pT_ev"], 4 * it + (s + 1)))
                    if reuse:
                        pe.wait_ge(*at(f["o_ev"], 4 * it + (s - 1)))
                    pT, bank, cols = pT_p[:, s % 2, :], 6 + s % 2, ds(4 * HD * it + HD * s, HD)
                    mm(ps[:, bank, 0:HD], pT[:, 0:P], kv_tok[:, 1, 0, cols], start=True, stop=True)
                    mm(ps[:, bank, HD:2 * HD], pT[:, P:2 * P], kv_tok[:, 1, 0, cols], start=True, stop=False)
                    mm(ps[:, bank, HD:2 * HD], pT[:, 2 * P:T], kv_tok[:, 1, 1, cols], start=False, stop=True).then_inc(
                        f["o"][0], 1)

                def prompt(it, s, live):
                    if live(0):
                        p_scores(it, s)
                    if live(-1):
                        p_turn(it, s - 1)
                    if live(-2):
                        p_out(it, s - 2, live(-4))

                pipeline(pe, HEADS, prompt, behind=2)
                pe.wait_ge(*at(f["o_ev"], HEADS))
                for k in range(KD):
                    for t in range(2):
                        ins = nc.tensor.transpose(ps[:, k, t * P:(t + 1) * P], o_tok[:, t, k * P:(k + 1) * P], ident[:, :])
                    ins.then_inc(f["oT"][0], 1)
                pe.wait_ge(*at(f["c"], 1 + DB))
                pe.wait_ge(*at(f["heads8"], 1))
                pe.wait_ge(*at(f["oT_lo"], KD))

                pe.wait_ge(mask_loaded, 16 * (KD + 3))
                def s_keys(it, s):
                    b2, hf = (s // 2) % 2, s % 2
                    if hf == 0:
                        pe.wait_ge(*at(f[f"k{b2}"], 16 * it + 16 * (s // 4 + 1)))
                    for g in range(4):
                        for n in range(2):
                            ins = nc.tensor.transpose(
                                ps[:, 2 * hf + g // 2, (g % 2) * PAST + n * P:(g % 2) * PAST + (n + 1) * P],
                                k_c[b2][:, n, (4 * hf + g) * P:(4 * hf + g + 1) * P], ident[:, :])
                    ins.then_inc(f["ktr"][0], 1)

                def s_scores(it, s):
                    b2, hf, bank = s // 2, s % 2, 4 + s % 2
                    if hf == 0:
                        pe.wait_ge(*at(f["qst"], 2 * it + (b2 + 1)))
                    pe.wait_ge(*at(f["kt_a"], 4 * it + (s + 1)))
                    pe.wait_ge(*at(f["kt_d"], 4 * it + (s + 1)))
                    for g in range(4):
                        rows, k = slice(32 * g, 32 * g + 32), 4 * hf + g
                        q = qbd[:, b2, k, :, :].rearrange("p e q -> p (e q)")
                        mm(ps[rows, bank, 0:PAST], q, ktc[:, k, :], start=True, stop=False, skip_group_check=True)
                    for g in range(4):
                        rows, k = slice(32 * g, 32 * g + 32), 4 * hf + g
                        q = qbd[:, b2, k, :, :].rearrange("p e q -> p (e q)")
                        mm(ps[rows, bank, PAST:PAST + DT], q, k_new[:, b2, k, :], start=False, stop=False,
                           skip_group_check=True)
                    mm(ps[:, bank, PAST:PAST + DT], ident[:, :], new_mask[:, :], start=False, stop=False,
                       skip_group_check=True)
                    mm(ps[:, bank, 0:PAST + DT].unsqueeze(1), heads8[:, hf, :], craw[:, ds(2 * it + b2, 1), :],
                       start=False, stop=True, skip_group_check=True).then_inc(f["s_scores"][0], 1)

                def s_turn(it, s):
                    pe.wait_ge(*at(f["s_exp"], 4 * it + (s + 1)))
                    for n in range(3):
                        ins = nc.tensor.transpose(ps[:, 6, n * P:(n + 1) * P], p_s[:, s % 2, n * P:(n + 1) * P], ident[:, :])
                    ins.then_inc(f["s_pT"][0], 1)

                def s_out(it, s, reuse):
                    b2, hf = (s // 2) % 2, s % 2
                    if hf == 0:
                        pe.wait_ge(*at(f[f"v{b2}"], 16 * it + 16 * (s // 4 + 1)))
                    pe.wait_ge(*at(f["s_pT_ev"], 4 * it + (s + 1)))
                    if reuse:
                        pe.wait_ge(*at(f["s_os"], 4 * it + s))
                    for n in range(3):
                        for g in range(4):
                            cols = slice((4 * hf + g) * P, (4 * hf + g + 1) * P)
                            v = kv_tok[:, 1, 2, cols] if n == 2 else v_c[b2][:, n, cols]
                            last = mm(ps[32 * g:32 * g + 32, 7, 0:P], pT_s[:, hf, n * P + 32 * g:n * P + 32 * g + 32], v,
                                      start=n == 0, stop=n == 2, skip_group_check=True)
                    last.then_inc(f["s_o"][0], 1)

                def s_fold(it, s):
                    pe.wait_ge(*at(f["s_x"], 4 * it + (s + 1)))
                    nc.tensor.transpose(ps[:, 7, P:2 * P], x_s[:, s % 2, :], ident[:, :]).then_inc(f["s_xT"][0], 1)

                def sample(it, s, live):
                    if live(-2):
                        s_fold(it, s - 2)
                    if iv(it) and 4 * it + s == 0:
                        s_keys(0, 0)
                    if live(1):
                        s_keys(it, s + 1)
                    if live(-1):
                        s_turn(it, s - 1)
                    if live(0):
                        s_scores(it, s)
                    if live(-1):
                        s_out(it, s - 1, live(-2))

                pipeline(pe, 2 * DB, sample, ahead=1, behind=2)
                pe.wait_ge(*at(f["s_lo"], 2 * DB))
                out_product(i)

            def hgrn(i, j):
                f, m0 = HGR[i], START[i]["mix"]
                for c in range(4):
                    if c >= 2:
                        pe.wait_ge(*at(f["ev"], c - 1))
                    for u in range(CU):
                        unit_fm(m0 + CU * c + u, 0, u, 4 * (c % 2), xT_hi, xT_lo, x_ready(2 * i) if c == 0 else None)
                with pe.Fori(0, 2) as w:
                    for h in range(2):
                        pe.wait_ge(*at(f["ev"], 2 * w + (h + 3)))
                        for u in range(CU):
                            unit_tm(m0 + (4 + h) * CU + u, 2 * w, u, 4 * h, xT_hi, xT_lo, KD)
                pe.wait_ge(*at(f["ev"], 8))

                def head(h, s):
                    col = ds(P * h, P)
                    first = iv(h) and h == 0
                    pe.wait_ge(*at(f["k2"], h + 1))
                    if not first:
                        pe.wait_ge(*at(f["sfin_ev"], h))
                    for t in range(NTOK):
                        ins = nc.tensor.transpose(ps[:, 4, t * P:(t + 1) * P], k2[:, t * P:(t + 1) * P], ident[:, :])
                    ins.then_inc(f["k2T"][0], 1)
                    pe.wait_ge(*at(f["lq"], h + 1))

                    def pairs(t):
                        tt, bank = slice(t * P, (t + 1) * P), 2 * (t % 2)
                        mm(ps[:, bank, 0:P].unsqueeze(1), k_h[:, s, tt], qT[:, ds(h, 1), tt], start=True, stop=True)
                        for n in range(TILE_LEVELS[t]):
                            side = lev[:, s, LOFF[n] + t * P:LOFF[n] + (t + 1) * P]
                            last = mm(ps[:, bank + (n + 1) // 4, ((n + 1) % 4) * P:((n + 1) % 4 + 1) * P], side, side,
                                      start=True, stop=True)
                        last.then_inc(f["sc"][0], 1)

                    def outputs(t):
                        pe.wait_ge(*at(f["scm"], NTOK * h + (t + 1)))
                        n = TILE_LEVELS[t] + 1
                        for l in range(n):
                            mm(ps[:, 5, t * P:(t + 1) * P], sc2[:, l, :] if t == 2 else sc[:, t, l, :], vg[:, 0, t, col], start=l == 0,
                               stop=t == 0 and l == n - 1)

                    pairs(0)
                    pairs(1)
                    pe.wait_ge(*at(f["k2T_ev"], h + 1))
                    mm(ps[:, 4, T:T + P], k2T[:, 0:P], vg[:, 0, 0, col], start=True, stop=True)
                    mm(ps[:, 4, 0:P], k2T[:, P:2 * P], vg[:, 0, 1, col], start=True, stop=True).then_inc(f["sfin"][0], 1)
                    pe.wait_ge(*at(f["scm"], NTOK * h + 1))
                    pairs(2)
                    if not first:
                        pe.wait_ge(*at(f["out"], h))
                    outputs(0)
                    outputs(1)
                    pe.wait_ge(*at(f["s1_ev"], h + 1))
                    mm(ps[:, 5, P:2 * P], q_e[:, s, P:2 * P], s1[:, :], start=False, stop=True)
                    outputs(2)
                    pe.wait_ge(*at(f["vm"], h + 1))
                    if not first:
                        pe.wait_ge(*at(f["snew"], h))
                    for a in range(2):
                        ins = mm(ps[:, 6 + a, :], k2T[:, 2 * P:T], v_m[:, 4 * a:4 * a + 4, :], start=True, stop=True)
                    ins.then_inc(f["upd"][0], 1)
                    turn = 8 * h + (16 - 8 * s)
                    pe.wait_ge(*at(f[f"st{s}_in"], turn))
                    pe.wait_ge(*at(f["qb"], h + 1))
                    for b in range(DB):
                        ins = mm(ps[:, 5, 2 * P:T], q_blk[:, s, b, :], S_b[:, s, b, :], start=False, stop=b == DB - 1)
                    ins.then_inc(f["o"][0], 1)

                head_pairs(pe, head)
                pe.wait_ge(*at(f["out"], HG))
                pe.wait_ge(*at(f["snew"], HG))
                for k in range(KD):
                    for t in range(NTOK):
                        ins = nc.tensor.transpose(ps[:, k, t * P:(t + 1) * P], vg[:, 0, t, k * P:(k + 1) * P], ident[:, :])
                    ins.then_inc(f["oT"][0], 1)
                pe.wait_ge(*at(f["oT_lo"], KD))
                out_product(i)

            def pool(i, j):
                f, m0 = POOL[i], START[i]["out"]
                pe.wait_ge(*at(f["ext"], 2 * KD))
                for h in range(2):
                    m = m0 + h
                    pe.wait_ge(lo_ready, m + 1)
                    for gg in range(2):
                        g = 2 * h + gg
                        pe.wait_ge(*at(f["lo"], g + 1))
                        for t in range(NTOK):
                            out, tt = ps[:, 4 * h + t, gg * 256:(gg + 1) * 256], slice(t * P, (t + 1) * P)
                            for kk in range(2):
                                cols = slice(kk * WCOLS + gg * 256, kk * WCOLS + (gg + 1) * 256)
                                k = 2 * g + kk
                                mm(out, xT_hi[:, k, tt], w_hi[:, m % RING, cols], start=kk == 0, stop=False)
                                mm(out, xT_hi[:, k, tt], w_lo[:, m % RING, cols], start=False, stop=False)
                                last = mm(out, xT_lo[:, k, tt], w_hi[:, m % RING, cols], start=False, stop=kk == 1)
                    last.then_inc(unit_used, 1)

            pe.wait_ge(ident_ready, 2)
            pe.wait_ge(rows_loaded, 48)
            for k in range(KD):
                nc.tensor.transpose(ps[:, 6, k * 4 * DEPTH:(k + 1) * 4 * DEPTH], gb_rows[:, k * P:(k + 1) * P],
                                    ident[0:4 * DEPTH, 0:4 * DEPTH])
                ins = nc.tensor.transpose(ps[:, 7, k * DEPTH:(k + 1) * DEPTH], lb_rows[:, k * P:(k + 1) * P],
                                          ident[0:DEPTH, 0:DEPTH])
            ins.then_inc(rowsT_done, 1)
            pe.wait_ge(gbT_ready, 2)
            transpose_x(0, x_tok, (x_loaded, 0))
            for i in range(DEPTH):
                kind = KINDS[i % 3]
                {"fox": fox, "hgrn": hgrn, "pool": pool}[kind](i, i // 3)
                pe.wait_ge(*at(LN[2 * i]["resid"], 2 * NTOK))
                transpose_x(2 * i + 1, xn, LN[2 * i]["xn"])
                ffn(i)
                if i + 1 < DEPTH:
                    pe.wait_ge(*at(LN[2 * i + 1]["resid"], 2 * NTOK))
                    if KINDS[(i + 1) % 3] == "pool":
                        pe.wait_ge(*at(POOL[i + 1]["in"], 32))
                        for k in range(KD):
                            nc.tensor.transpose(ps[:, k, T:T + DB * HIST], hist[:, k * P:(k + 1) * P],
                                                ident[0:DB * HIST, 0:DB * HIST])
                    transpose_x(2 * i + 2, xn, LN[2 * i + 1]["xn"])


_INS = ["x_prompt", "x_sample", "cache_fox_k", "cache_fox_v", "cache_fox_lf", "state_hgrn", "cache_pool",
        "w_fox_in", "b_fox_f", "w_fox_out", "w_hgrn_in", "hgrn_lb", "hgrn_norm_g", "w_hgrn_out",
        "w_pool", "pool_scale", "w_ffn_in", "w_ffn_out", "ln_g", "ln_b"]
_OUTS = [(1, 256, 1024), (8, 16, 1024), (2, 1, 256, 16, 64), (2, 1, 256, 16, 64), (2, 1, 256, 16), (1, 1, 8, 128, 128),
         (1, 1, 15, 1024), (2, 8, 16, 16, 64), (2, 8, 16, 16, 64), (2, 8, 16, 16), (1, 8, 8, 128, 128), (1, 8, 15, 1024)]


def kernel(**inputs):
    import numpy as _np
    import concourse.bacc as _bacc
    from concourse import mybir as _mybir
    from concourse.bass_utils import run_bass_kernel_spmd as _run

    nc = _bacc.Bacc("TRN2", target_bir_lowering=False, num_devices=1)
    arrays, args = {}, []
    for name in _INS:
        a = _np.ascontiguousarray(inputs[name])
        arrays[f"in_{name}_dram"] = a
        args.append(nc.dram_tensor(f"in_{name}_dram", a.shape, _mybir.dt.from_np(a.dtype), kind="ExternalInput").ap())
    for i, shape in enumerate(_OUTS):
        args.append(nc.dram_tensor(f"out_{i}_dram", shape, _mybir.dt.float32, kind="ExternalOutput").ap())
    trunk_program(nc, *args)
    r = _run(nc, [arrays], core_ids=[0])
    return tuple(r.results[0][f"out_{i}_dram"] for i in range(len(_OUTS)))
```
